# Optimizing a Trainium2 kernel written in Bass

```python
import math
import jax, jax.numpy as jnp
from jax import lax
import numpy as np

D_MODEL = 1024
BATCH = 1
SEQ = 2048
DEPTH = 1

PLE_DIM = 256
HEAD_DIM = 64
DIFF_HEADS = 4
DIFF_QK = 2 * HEAD_DIM
DIFF_V = 2 * HEAD_DIM
DIFF_WIDTH = DIFF_HEADS * DIFF_V
DIL_HEADS = 8
DIL_WIDTH = DIL_HEADS * HEAD_DIM
DIL_PATTERNS = ((128, 1), (512, 4), (2048, 16))
MIX_WIDTH = DIFF_WIDTH + DIL_WIDTH
Q_BLOCK = 128
NORM_EPS = 1e-6
MASK_VALUE = -1e30

IN_SPLIT_SIZES = (
    DIFF_HEADS * DIFF_QK,
    DIFF_HEADS * DIFF_QK,
    DIFF_WIDTH,
    DIL_WIDTH,
    DIL_WIDTH,
    DIL_WIDTH,
    MIX_WIDTH,
)
IN_WIDTH = sum(IN_SPLIT_SIZES)
IN_SPLIT_IDX = tuple(int(v) for v in np.cumsum(IN_SPLIT_SIZES)[:-1])


def rms_norm(t, g):
    tf = t.astype(jnp.float32)
    y = tf * lax.rsqrt(jnp.mean(tf * tf, axis=-1, keepdims=True) + NORM_EPS)
    return (y * g.astype(jnp.float32)).astype(t.dtype)

def alibi_slopes(n_heads):
    return jnp.exp2(-8.0 * jnp.arange(1, n_heads + 1, dtype=jnp.float32) / n_heads)

def diff_attention(q, k, v, lam, slopes):
    B, S, H, _, Dh = q.shape
    scale = Dh ** -0.5
    nqb = S // Q_BLOCK
    pos = jnp.arange(S)
    qb = q.reshape(B, nqb, Q_BLOCK, H, 2, Dh).transpose(1, 0, 2, 3, 4, 5)
    qpos = pos.reshape(nqb, Q_BLOCK)

    def block(args):
        qblk, qp = args
        s = jnp.einsum('bqhce,bkhce->bchqk', qblk, k).astype(jnp.float32) * scale
        dist = jnp.abs(qp[:, None] - pos[None, :]).astype(jnp.float32)
        s = s - slopes[:, None, None] * dist
        a = jax.nn.softmax(s, axis=-1)
        w = a[:, 0] - lam * a[:, 1]
        return jnp.einsum('bhqk,bkhe->bqhe', w.astype(v.dtype), v)

    out = lax.map(block, (qb, qpos))
    return out.transpose(1, 0, 2, 3, 4).reshape(B, S, H, 2 * Dh)

def dilated_branch(q, k, v, slopes, window, dilation):
    B, S, H, Dh = q.shape
    r = window // (2 * dilation)
    blk = r
    unit = dilation * blk
    Lp = -(-S // unit) * unit
    n = Lp // dilation
    nb = n // blk
    scale = Dh ** -0.5

    def split(t):
        t = jnp.pad(t, ((0, 0), (0, Lp - S), (0, 0), (0, 0)))
        return t.reshape(B, nb, blk, dilation, H, Dh)

    def window3(t):
        tp = jnp.pad(t, ((0, 0), (1, 1), (0, 0), (0, 0), (0, 0), (0, 0)))
        return jnp.concatenate([tp[:, :-2], tp[:, 1:-1], tp[:, 2:]], axis=2)

    qs = split(q)
    kw = window3(split(k))
    vw = window3(split(v))

    qi = jnp.arange(nb)[:, None] * blk + jnp.arange(blk)[None, :]
    kj = (jnp.arange(nb)[:, None] - 1) * blk + jnp.arange(3 * blk)[None, :]
    rel = qi[:, :, None] - kj[:, None, :]
    kpos = kj[:, :, None] * dilation + jnp.arange(dilation)[None, None, :]
    key_ok = ((kj >= 0)[:, :, None] & (kpos < S)).transpose(0, 2, 1)
    mask = (jnp.abs(rel) <= r)[:, None, None] & key_ok[:, :, None, None, :]
    dist = (dilation * jnp.abs(rel)).astype(jnp.float32)[:, None, None]
    bias = -slopes[:, None, None] * dist

    s = jnp.einsum('bnqche,bnkche->bnchqk', qs, kw).astype(jnp.float32) * scale + bias
    s = jnp.where(mask, s, MASK_VALUE)
    m = jnp.max(s, axis=-1, keepdims=True)
    e = jnp.exp(s - m)
    l = jnp.sum(e, axis=-1, keepdims=True)
    o = jnp.einsum('bnchqk,bnkche->bnqche', e.astype(v.dtype), vw)
    inv_l = (1.0 / l[..., 0]).transpose(0, 1, 4, 2, 3)[..., None]
    o = (o.astype(jnp.float32) * inv_l).reshape(B, Lp, H, Dh)[:, :S]
    lse = (m[..., 0] + jnp.log(l[..., 0])).transpose(0, 1, 4, 2, 3).reshape(B, Lp, H)[:, :S]
    return o, lse

def dilated_attention(q, k, v, slopes):
    outs, lses = [], []
    for window, dilation in DIL_PATTERNS:
        o, lse = dilated_branch(q, k, v, slopes, window, dilation)
        outs.append(o)
        lses.append(lse)
    w = jax.nn.softmax(jnp.stack(lses, axis=0), axis=0)
    out = jnp.sum(w[..., None] * jnp.stack(outs, axis=0), axis=0)
    return out.astype(q.dtype)

def first_inputs(seed: int = 0) -> dict:
    key = jax.random.key(seed)
    ks = jax.random.split(key, 20)
    f32 = jnp.float32

    def gain(k, n):
        return 1.0 + 0.02 * jax.random.normal(k, (DEPTH, n), f32)

    return {
        "x": jax.random.normal(ks[0], (BATCH, SEQ, D_MODEL), f32),
        "p": jax.random.normal(ks[1], (DEPTH, BATCH, SEQ, PLE_DIM), f32),
        "mix_norm_g": gain(ks[2], D_MODEL),
        "w_in": jax.random.normal(ks[3], (DEPTH, D_MODEL, IN_WIDTH), f32) * D_MODEL ** -0.5,
        "diff_q_norm_g": gain(ks[4], HEAD_DIM),
        "diff_k_norm_g": gain(ks[5], HEAD_DIM),
        "lambda_q1": 0.1 * jax.random.normal(ks[6], (DEPTH, HEAD_DIM), f32),
        "lambda_k1": 0.1 * jax.random.normal(ks[7], (DEPTH, HEAD_DIM), f32),
        "lambda_q2": 0.1 * jax.random.normal(ks[8], (DEPTH, HEAD_DIM), f32),
        "lambda_k2": 0.1 * jax.random.normal(ks[9], (DEPTH, HEAD_DIM), f32),
        "diff_sub_norm_g": gain(ks[10], DIFF_V),
        "dil_q_norm_g": gain(ks[11], HEAD_DIM),
        "dil_k_norm_g": gain(ks[12], HEAD_DIM),
        "w_out": jax.random.normal(ks[13], (DEPTH, MIX_WIDTH, D_MODEL), f32) * MIX_WIDTH ** -0.5,
        "ple_norm_g": gain(ks[14], D_MODEL),
        "w_ple_gate": jax.random.normal(ks[15], (DEPTH, D_MODEL, D_MODEL), f32) * D_MODEL ** -0.5,
        "w_ple_proj": jax.random.normal(ks[16], (DEPTH, PLE_DIM, D_MODEL), f32) * PLE_DIM ** -0.5,
    }

def first_block(x, p, mix_norm_g, w_in, diff_q_norm_g, diff_k_norm_g,
              lambda_q1, lambda_k1, lambda_q2, lambda_k2, diff_sub_norm_g,
              dil_q_norm_g, dil_k_norm_g, w_out, ple_norm_g, w_ple_gate, w_ple_proj):
    B, S, _ = x.shape
    diff_slopes = alibi_slopes(DIFF_HEADS)
    dil_slopes = alibi_slopes(DIL_HEADS)
    for i in range(DEPTH):
        lam_init = 0.8 - 0.6 * math.exp(-0.3 * i)
        h = rms_norm(x, mix_norm_g[i])
        u = h @ w_in[i]
        dq, dk, dv, bq, bk, bv, z = jnp.split(u, IN_SPLIT_IDX, axis=-1)

        dq = rms_norm(dq.reshape(B, S, DIFF_HEADS, 2, HEAD_DIM), diff_q_norm_g[i])
        dk = rms_norm(dk.reshape(B, S, DIFF_HEADS, 2, HEAD_DIM), diff_k_norm_g[i])
        dv = dv.reshape(B, S, DIFF_HEADS, DIFF_V)
        lam = (jnp.exp(jnp.sum(lambda_q1[i].astype(jnp.float32) * lambda_k1[i].astype(jnp.float32)))
               - jnp.exp(jnp.sum(lambda_q2[i].astype(jnp.float32) * lambda_k2[i].astype(jnp.float32)))
               + lam_init)
        a = diff_attention(dq, dk, dv, lam, diff_slopes)
        a = rms_norm(a, diff_sub_norm_g[i]) * (1.0 - lam_init)
        a = a.reshape(B, S, DIFF_WIDTH)

        bq = rms_norm(bq.reshape(B, S, DIL_HEADS, HEAD_DIM), dil_q_norm_g[i])
        bk = rms_norm(bk.reshape(B, S, DIL_HEADS, HEAD_DIM), dil_k_norm_g[i])
        bv = bv.reshape(B, S, DIL_HEADS, HEAD_DIM)
        b = dilated_attention(bq, bk, bv, dil_slopes).reshape(B, S, DIL_WIDTH)

        y = jnp.concatenate([a, b], axis=-1) * jax.nn.silu(z)
        x = x + y @ w_out[i]

        gate = jax.nn.sigmoid(rms_norm(x, ple_norm_g[i]) @ w_ple_gate[i])
        x = x + gate * (p[i] @ w_ple_proj[i])
    return x


N_MIXERS = 4
EPS = 1e-6
NEG = -1e30
BIG = 1e30
T5_BUCKETS = 32
T5_MAX_DIST = 128
ATTN_HEADS = 16
HEAD_DIM_2 = D_MODEL // ATTN_HEADS
KV_HEADS = 4
GQA = ATTN_HEADS // KV_HEADS
SWA_WINDOW = 128
RWKV_HEAD = 64
RWKV_HEADS = D_MODEL // RWKV_HEAD
RWKV_LORA_W = 64
RWKV_LORA_A = 64
RWKV_GN_EPS = 64e-5
NSA_CMP_LEN = 32
NSA_CMP_STRIDE = 16
NSA_CMP_HIDDEN = 128
NSA_SEL_LEN = 64
NSA_TOPK = 16
NSA_WINDOW = 512
NSA_SEL_QCHUNK = 64
LRU_WIDTH = 1280
LRU_BLOCKS = 16
LRU_BLOCK = LRU_WIDTH // LRU_BLOCKS
LRU_C = 8.0
CONV_WIDTH = 4


def _layers_of(m):
    return len(range(m, DEPTH, N_MIXERS))

def rms_norm_2(x, g):
    xf = x.astype(jnp.float32)
    y = xf * lax.rsqrt(jnp.mean(xf * xf, axis=-1, keepdims=True) + EPS)
    return (y * g.astype(jnp.float32)).astype(x.dtype)

def t5_bucket(dist):
    max_exact = T5_BUCKETS // 2
    d = jnp.maximum(dist, 0)
    df = jnp.maximum(d, 1).astype(jnp.float32)
    large = max_exact + (jnp.log(df / max_exact) / math.log(T5_MAX_DIST / max_exact)
                         * (T5_BUCKETS - max_exact)).astype(jnp.int32)
    large = jnp.minimum(large, T5_BUCKETS - 1)
    return jnp.where(d < max_exact, d, large)

def q_heads(t, B, T):
    return t.reshape(B, T, KV_HEADS, GQA, HEAD_DIM_2).transpose(0, 2, 3, 1, 4)

def kv_heads(t, B, T):
    return t.reshape(B, T, KV_HEADS, HEAD_DIM_2).transpose(0, 2, 1, 3)

def merge_heads(o, B, T):
    return o.transpose(0, 3, 1, 2, 4).reshape(B, T, ATTN_HEADS * HEAD_DIM_2)

def banded_attention(q, k, v, t5_table, window, sinks=None):
    B, G, R, T, Dh = q.shape
    nb = T // Q_BLOCK
    nprev = -(-window // Q_BLOCK)
    kc = (nprev + 1) * Q_BLOCK
    qb = q.reshape(B, G, R, nb, Q_BLOCK, Dh)
    pad = ((0, 0), (0, 0), (nprev * Q_BLOCK, 0), (0, 0))
    kp = jnp.pad(k, pad).reshape(B, G, nb + nprev, Q_BLOCK, Dh)
    vp = jnp.pad(v, pad).reshape(B, G, nb + nprev, Q_BLOCK, Dh)
    kb = jnp.concatenate([kp[:, :, j:j + nb] for j in range(nprev + 1)], axis=3)
    vb = jnp.concatenate([vp[:, :, j:j + nb] for j in range(nprev + 1)], axis=3)
    s = jnp.einsum('bgrnqd,bgnkd->bgrnqk', qb, kb,
                   preferred_element_type=jnp.float32) * (Dh ** -0.5)
    dist = nprev * Q_BLOCK + jnp.arange(Q_BLOCK)[:, None] - jnp.arange(kc)[None, :]
    kpos = (jnp.arange(nb)[:, None, None] - nprev) * Q_BLOCK + jnp.arange(kc)[None, None, :]
    valid = (dist >= 0) & (dist < window) & (kpos >= 0)
    bias = jnp.take(t5_table, t5_bucket(dist), axis=0)
    bias = jnp.moveaxis(bias, -1, 0).reshape(G, R, Q_BLOCK, kc).astype(jnp.float32)
    s = jnp.where(valid, s + bias[None, :, :, None], NEG)
    if sinks is None:
        p = jax.nn.softmax(s, axis=-1)
    else:
        sk = jnp.broadcast_to(sinks.astype(jnp.float32).reshape(1, G, R, 1, 1, 1), s.shape[:-1] + (1,))
        p = jax.nn.softmax(jnp.concatenate([s, sk], axis=-1), axis=-1)[..., :-1]
    o = jnp.einsum('bgrnqk,bgnkd->bgrnqd', p.astype(v.dtype), vb)
    return o.reshape(B, G, R, T, Dh)

def swa_sink_mixer(xn, w_in, sinks, w_out, t5_table):
    B, T, _ = xn.shape
    nq, nkv = ATTN_HEADS * HEAD_DIM_2, KV_HEADS * HEAD_DIM_2
    q, k, v, z = jnp.split(xn @ w_in, [nq, nq + nkv, nq + 2 * nkv], axis=-1)
    o = banded_attention(q_heads(q, B, T), kv_heads(k, B, T), kv_heads(v, B, T),
                         t5_table, SWA_WINDOW, sinks)
    return (merge_heads(o, B, T) * jax.nn.silu(z)) @ w_out

def rwkv7_mixer(xn, mu, w_in, w0, w1, w2, a0, a1, a2, k_k, k_a, r_k, lnx_w, lnx_b, w_out):
    B, T, D = xn.shape
    H, N = RWKV_HEADS, RWKV_HEAD
    C = H * N
    f32 = jnp.float32
    xx = jnp.pad(xn, ((0, 0), (1, 0), (0, 0)))[:, :-1] - xn
    lerp = xn[None] + xx[None] * mu[:, None, None, :]
    rkvz = jnp.einsum('sbtd,dsc->sbtc', lerp[:4], w_in.reshape(D, 4, C))
    r, k, v, z = rkvz[0], rkvz[1], rkvz[2], rkvz[3]
    w = -jax.nn.softplus(-(w0 + jnp.tanh(lerp[4] @ w1) @ w2)) - 0.5
    a = jax.nn.sigmoid(a0 + (lerp[5] @ a1) @ a2)
    hs = lambda t: t.astype(f32).reshape(B, T, H, N)
    kk = hs(k * k_k)
    kk = kk / jnp.maximum(jnp.sqrt(jnp.sum(kk * kk, axis=-1, keepdims=True)), 1e-12)
    k = hs(k * (1 + (a - 1) * k_a))
    r, v, a = hs(r), hs(v), hs(a)
    decay = jnp.exp(-jnp.exp(hs(w)))
    aa, bb = -kk, kk * a

    def step(S, inp):
        r_t, w_t, k_t, v_t, a_t, b_t = inp
        sa = jnp.einsum('bhij,bhj->bhi', S, a_t)
        S = S * w_t[:, :, None, :] + sa[..., None] * b_t[:, :, None, :] + v_t[..., None] * k_t[:, :, None, :]
        return S, jnp.einsum('bhij,bhj->bhi', S, r_t)

    xs = tuple(jnp.moveaxis(t, 1, 0) for t in (r, decay, k, v, aa, bb))
    _, y = lax.scan(step, jnp.zeros((B, H, N, N), f32), xs)
    y = jnp.moveaxis(y, 0, 1)
    mean = jnp.mean(y, axis=-1, keepdims=True)
    var = jnp.mean(jnp.square(y - mean), axis=-1, keepdims=True)
    y = ((y - mean) * lax.rsqrt(var + RWKV_GN_EPS)).reshape(B, T, C) * lnx_w.astype(f32) + lnx_b.astype(f32)
    bonus = jnp.sum(r * k * r_k.astype(f32), axis=-1, keepdims=True) * v
    y = (y + bonus.reshape(B, T, C)) * jax.nn.silu(z.astype(f32))
    return y.astype(xn.dtype) @ w_out

def nsa_mixer(xn, w_in, cmp_pos_k, cmp_k_w1, cmp_k_w2, cmp_pos_v, cmp_v_w1, cmp_v_w2, w_out, t5_table):
    B, T, _ = xn.shape
    G, R, Dh = KV_HEADS, GQA, HEAD_DIM_2
    f32 = jnp.float32
    nq, nkv = ATTN_HEADS * Dh, G * Dh
    splits = np.cumsum([nq] + [nkv] * 6 + [3 * ATTN_HEADS]).tolist()
    q, kc, vc, ks, vs, kw, vw, gates, z = jnp.split(xn @ w_in, splits, axis=-1)
    q = q_heads(q, B, T)
    kc, vc, ks, vs, kw, vw = (kv_heads(t, B, T) for t in (kc, vc, ks, vs, kw, vw))
    scale = Dh ** -0.5
    tpos = jnp.arange(T)

    n_cmp = (T - NSA_CMP_LEN) // NSA_CMP_STRIDE + 1
    tok_idx = np.arange(n_cmp)[:, None] * NSA_CMP_STRIDE + np.arange(NSA_CMP_LEN)[None, :]

    def compress(t, pos, w1, w2):
        blk = (t[:, :, tok_idx] + pos).reshape(B, G, n_cmp, NSA_CMP_LEN * Dh)
        return jax.nn.silu(blk @ w1) @ w2

    k_cmp = compress(kc, cmp_pos_k, cmp_k_w1, cmp_k_w2)
    v_cmp = compress(vc, cmp_pos_v, cmp_v_w1, cmp_v_w2)
    cmp_start = jnp.arange(n_cmp) * NSA_CMP_STRIDE
    cmp_end = cmp_start + NSA_CMP_LEN - 1
    cmp_ok = cmp_end[None, :] <= tpos[:, None]
    s_c = jnp.einsum('bgrtd,bgnd->bgrtn', q, k_cmp, preferred_element_type=f32) * scale
    p_c = jax.nn.softmax(jnp.where(cmp_ok, s_c, NEG), axis=-1) * cmp_ok
    o_cmp = jnp.einsum('bgrtn,bgnd->bgrtd', p_c.astype(v_cmp.dtype), v_cmp)

    n_sel = T // NSA_SEL_LEN
    k_top = min(NSA_TOPK, n_sel)
    sel_start = jnp.arange(n_sel) * NSA_SEL_LEN
    overlap = ((cmp_start[:, None] < sel_start[None, :] + NSA_SEL_LEN)
               & (cmp_end[:, None] >= sel_start[None, :])).astype(f32)
    imp = jnp.einsum('bgrtn,ns->bgts', p_c, overlap)
    blk = jnp.arange(n_sel)[None, :]
    cur = (tpos // NSA_SEL_LEN)[:, None]
    forced = (blk == 0) | (blk == cur) | (blk == cur - 1)
    future = sel_start[None, :] > tpos[:, None]
    imp = jnp.where(forced, BIG, jnp.where(future, NEG, imp))
    _, sel_idx = lax.top_k(imp, k_top)

    ks_blk = ks.reshape(B, G, n_sel, NSA_SEL_LEN, Dh)
    vs_blk = vs.reshape(B, G, n_sel, NSA_SEL_LEN, Dh)
    QC = NSA_SEL_QCHUNK
    nch = T // QC
    q_ch = jnp.moveaxis(q.reshape(B, G, R, nch, QC, Dh), 3, 0)
    idx_ch = jnp.moveaxis(sel_idx.reshape(B, G, nch, QC, k_top), 2, 0)
    pos_ch = tpos.reshape(nch, QC)
    bi = jnp.arange(B)[:, None, None, None]
    gi = jnp.arange(G)[None, :, None, None]
    gi5 = jnp.arange(G)[None, :, None, None, None]
    table_g = t5_table.reshape(T5_BUCKETS, G, R)

    def sel_chunk(args):
        qc, ic, pc = args
        kg = ks_blk[bi, gi, ic]
        vg = vs_blk[bi, gi, ic]
        kpos = ic[..., None] * NSA_SEL_LEN + jnp.arange(NSA_SEL_LEN)
        dist = pc[None, None, :, None, None] - kpos
        s = jnp.einsum('bgrqd,bgqskd->bgrqsk', qc, kg, preferred_element_type=f32) * scale
        bias = jnp.moveaxis(table_g[t5_bucket(dist), gi5], -1, 2).astype(f32)
        s = jnp.where((dist >= 0)[:, :, None], s + bias, NEG)
        p = jax.nn.softmax(s.reshape(B, G, R, QC, k_top * NSA_SEL_LEN), axis=-1)
        p = p.reshape(B, G, R, QC, k_top, NSA_SEL_LEN)
        return jnp.einsum('bgrqsk,bgqskd->bgrqd', p.astype(vg.dtype), vg)

    o_sel = lax.map(sel_chunk, (q_ch, idx_ch, pos_ch))
    o_sel = jnp.moveaxis(o_sel, 0, 3).reshape(B, G, R, T, Dh)

    o_win = banded_attention(q, kw, vw, t5_table, NSA_WINDOW)

    g = jax.nn.sigmoid(gates).reshape(B, T, 3, G, R).transpose(2, 0, 3, 4, 1)[..., None]
    o = g[0] * o_cmp + g[1] * o_sel + g[2] * o_win
    return (merge_heads(o, B, T) * jax.nn.silu(z)) @ w_out

def rglru_mixer(xn, w_in, conv_w, conv_b, gate_a_w, gate_a_b, gate_x_w, gate_x_b, lam, w_out):
    B, T, _ = xn.shape
    f32 = jnp.float32
    u, z = jnp.split(xn @ w_in, 2, axis=-1)
    u = lax.conv_general_dilated(u, conv_w[:, None, :], window_strides=(1,),
                                 padding=[(CONV_WIDTH - 1, 0)],
                                 dimension_numbers=('NWC', 'WIO', 'NWC'),
                                 feature_group_count=LRU_WIDTH) + conv_b
    ub = u.reshape(B, T, LRU_BLOCKS, LRU_BLOCK)
    r = jax.nn.sigmoid(jnp.einsum('btnc,ncd->btnd', ub, gate_a_w).reshape(B, T, LRU_WIDTH) + gate_a_b)
    i = jax.nn.sigmoid(jnp.einsum('btnc,ncd->btnd', ub, gate_x_w).reshape(B, T, LRU_WIDTH) + gate_x_b)
    log_a = -LRU_C * r.astype(f32) * jax.nn.softplus(-lam.astype(f32))
    a = jnp.exp(log_a)
    b = jnp.sqrt(-jnp.expm1(2.0 * log_a)) * (i * u).astype(f32)

    def combine(left, right):
        a1, b1 = left
        a2, b2 = right
        return a1 * a2, a2 * b1 + b2

    _, h = lax.associative_scan(combine, (a, b), axis=1)
    return (h.astype(xn.dtype) * jax.nn.silu(z)) @ w_out

def second_inputs(seed: int = 0) -> dict:
    key = jax.random.key(seed)
    keys = iter(jax.random.split(key, 64))
    f32 = jnp.float32

    def nrm(shape, scale):
        return jax.random.normal(next(keys), shape, f32) * scale

    def dense(shape):
        return nrm(shape, shape[-2] ** -0.5)

    def unif(shape, lo, hi):
        return jax.random.uniform(next(keys), shape, f32, lo, hi)

    LA, LB, LC, LD = (_layers_of(m) for m in range(N_MIXERS))
    C = RWKV_HEADS * RWKV_HEAD
    nq, nkv = ATTN_HEADS * HEAD_DIM_2, KV_HEADS * HEAD_DIM_2
    a_cols = 2 * nq + 2 * nkv
    c_cols = 2 * nq + 6 * nkv + 3 * ATTN_HEADS
    lam_u = unif((LD, LRU_WIDTH), 0.9, 0.999)
    return {
        "x": nrm((BATCH, SEQ, D_MODEL), 1.0),
        "t5_table": nrm((T5_BUCKETS, ATTN_HEADS), 0.5),
        "norm_g": 1.0 + nrm((DEPTH, D_MODEL), 0.05),
        "final_g": 1.0 + nrm((D_MODEL,), 0.05),
        "a_w_in": dense((LA, D_MODEL, a_cols)),
        "a_sinks": nrm((LA, ATTN_HEADS), 0.5),
        "a_w_out": dense((LA, nq, D_MODEL)),
        "b_mu": unif((LB, 6, D_MODEL), 0.0, 1.0),
        "b_w_in": dense((LB, D_MODEL, 4 * C)),
        "b_w0": unif((LB, C), -6.0, 0.0),
        "b_w1": dense((LB, D_MODEL, RWKV_LORA_W)),
        "b_w2": dense((LB, RWKV_LORA_W, C)),
        "b_a0": nrm((LB, C), 0.5),
        "b_a1": dense((LB, D_MODEL, RWKV_LORA_A)),
        "b_a2": dense((LB, RWKV_LORA_A, C)),
        "b_k_k": 0.85 + nrm((LB, C), 0.1),
        "b_k_a": 1.0 + nrm((LB, C), 0.1),
        "b_r_k": nrm((LB, RWKV_HEADS, RWKV_HEAD), 0.1),
        "b_lnx_w": 1.0 + nrm((LB, C), 0.05),
        "b_lnx_b": nrm((LB, C), 0.01),
        "b_w_out": dense((LB, C, D_MODEL)),
        "c_w_in": dense((LC, D_MODEL, c_cols)),
        "c_cmp_pos_k": nrm((LC, NSA_CMP_LEN, HEAD_DIM_2), 0.1),
        "c_cmp_k_w1": dense((LC, NSA_CMP_LEN * HEAD_DIM_2, NSA_CMP_HIDDEN)),
        "c_cmp_k_w2": dense((LC, NSA_CMP_HIDDEN, HEAD_DIM_2)),
        "c_cmp_pos_v": nrm((LC, NSA_CMP_LEN, HEAD_DIM_2), 0.1),
        "c_cmp_v_w1": dense((LC, NSA_CMP_LEN * HEAD_DIM_2, NSA_CMP_HIDDEN)),
        "c_cmp_v_w2": dense((LC, NSA_CMP_HIDDEN, HEAD_DIM_2)),
        "c_w_out": dense((LC, nq, D_MODEL)),
        "d_w_in": dense((LD, D_MODEL, 2 * LRU_WIDTH)),
        "d_conv_w": nrm((LD, CONV_WIDTH, LRU_WIDTH), CONV_WIDTH ** -0.5),
        "d_conv_b": nrm((LD, LRU_WIDTH), 0.01),
        "d_gate_a_w": dense((LD, LRU_BLOCKS, LRU_BLOCK, LRU_BLOCK)),
        "d_gate_a_b": nrm((LD, LRU_WIDTH), 0.01),
        "d_gate_x_w": dense((LD, LRU_BLOCKS, LRU_BLOCK, LRU_BLOCK)),
        "d_gate_x_b": nrm((LD, LRU_WIDTH), 0.01),
        "d_lambda": jnp.log(lam_u) - jnp.log1p(-lam_u),
        "d_w_out": dense((LD, LRU_WIDTH, D_MODEL)),
    }

def second_block(x, t5_table, norm_g, final_g,
              a_w_in, a_sinks, a_w_out,
              b_mu, b_w_in, b_w0, b_w1, b_w2, b_a0, b_a1, b_a2, b_k_k, b_k_a, b_r_k,
              b_lnx_w, b_lnx_b, b_w_out,
              c_w_in, c_cmp_pos_k, c_cmp_k_w1, c_cmp_k_w2, c_cmp_pos_v, c_cmp_v_w1, c_cmp_v_w2, c_w_out,
              d_w_in, d_conv_w, d_conv_b, d_gate_a_w, d_gate_a_b, d_gate_x_w, d_gate_x_b,
              d_lambda, d_w_out):
    for layer in range(DEPTH):
        m, j = layer % N_MIXERS, layer // N_MIXERS
        xn = rms_norm_2(x, norm_g[layer])
        if m == 0:
            y = swa_sink_mixer(xn, a_w_in[j], a_sinks[j], a_w_out[j], t5_table)
        elif m == 1:
            y = rwkv7_mixer(xn, b_mu[j], b_w_in[j], b_w0[j], b_w1[j], b_w2[j], b_a0[j], b_a1[j],
                            b_a2[j], b_k_k[j], b_k_a[j], b_r_k[j], b_lnx_w[j], b_lnx_b[j], b_w_out[j])
        elif m == 2:
            y = nsa_mixer(xn, c_w_in[j], c_cmp_pos_k[j], c_cmp_k_w1[j], c_cmp_k_w2[j],
                          c_cmp_pos_v[j], c_cmp_v_w1[j], c_cmp_v_w2[j], c_w_out[j], t5_table)
        else:
            y = rglru_mixer(xn, d_w_in[j], d_conv_w[j], d_conv_b[j], d_gate_a_w[j], d_gate_a_b[j],
                            d_gate_x_w[j], d_gate_x_b[j], d_lambda[j], d_w_out[j])
        x = x + y.astype(x.dtype)
    return rms_norm_2(x, final_g)


def setup_inputs(seed=0):
    out = dict(first_inputs(seed))
    for name, value in second_inputs(seed + 1).items():
        if name != "x":
            out[name + "_2"] = value
    return out


def reference(
    x, p, mix_norm_g, w_in, diff_q_norm_g, diff_k_norm_g, lambda_q1, lambda_k1, lambda_q2,
    lambda_k2, diff_sub_norm_g, dil_q_norm_g, dil_k_norm_g, w_out, ple_norm_g, w_ple_gate,
    w_ple_proj, t5_table_2, norm_g_2, final_g_2, a_w_in_2, a_sinks_2, a_w_out_2, b_mu_2,
    b_w_in_2, b_w0_2, b_w1_2, b_w2_2, b_a0_2, b_a1_2, b_a2_2, b_k_k_2, b_k_a_2, b_r_k_2,
    b_lnx_w_2, b_lnx_b_2, b_w_out_2, c_w_in_2, c_cmp_pos_k_2, c_cmp_k_w1_2, c_cmp_k_w2_2,
    c_cmp_pos_v_2, c_cmp_v_w1_2, c_cmp_v_w2_2, c_w_out_2, d_w_in_2, d_conv_w_2, d_conv_b_2,
    d_gate_a_w_2, d_gate_a_b_2, d_gate_x_w_2, d_gate_x_b_2, d_lambda_2, d_w_out_2,
):
    x = first_block(
        x, p, mix_norm_g, w_in, diff_q_norm_g, diff_k_norm_g, lambda_q1, lambda_k1, lambda_q2,
        lambda_k2, diff_sub_norm_g, dil_q_norm_g, dil_k_norm_g, w_out, ple_norm_g, w_ple_gate,
        w_ple_proj,
    )
    return second_block(
        x, t5_table_2, norm_g_2, final_g_2, a_w_in_2, a_sinks_2, a_w_out_2, b_mu_2, b_w_in_2,
        b_w0_2, b_w1_2, b_w2_2, b_a0_2, b_a1_2, b_a2_2, b_k_k_2, b_k_a_2, b_r_k_2, b_lnx_w_2,
        b_lnx_b_2, b_w_out_2, c_w_in_2, c_cmp_pos_k_2, c_cmp_k_w1_2, c_cmp_k_w2_2,
        c_cmp_pos_v_2, c_cmp_v_w1_2, c_cmp_v_w2_2, c_w_out_2, d_w_in_2, d_conv_w_2, d_conv_b_2,
        d_gate_a_w_2, d_gate_a_b_2, d_gate_x_w_2, d_gate_x_b_2, d_lambda_2, d_w_out_2,
    )


_drawn_inputs = setup_inputs


def setup_inputs(seed=0):
    import zlib

    import numpy as np

    out = dict(_drawn_inputs(seed))
    spreads = {}
    factors = {'mix_norm_g': 4.568,
     'diff_q_norm_g': 8.0,
     'diff_k_norm_g': 8.0,
     'lambda_q1': 7.343,
     'lambda_k2': 8.0,
     'diff_sub_norm_g': 8.0,
     'dil_q_norm_g': 8.0,
     'dil_k_norm_g': 8.0,
     'ple_norm_g': 200.0,
     'norm_g_2': 6.755,
     'a_sinks_2': 64.0}
    for name, (base, spread) in spreads.items():
        noise = np.random.default_rng([zlib.crc32(name.encode()), seed]).standard_normal(out[name].shape)
        drawn = base * np.exp(spread * noise) if base else spread * noise
        out[name] = __import__('jax').numpy.asarray(drawn.astype(out[name].dtype))
    for name, factor in factors.items():
        out[name] = (out[name] * factor).astype(out[name].dtype)
    return out
```

```python
import math
from contextlib import ExitStack

import numpy as np

import concourse.bass as bass
from concourse import mybir

ALU = mybir.AluOpType
ACT = mybir.ActivationFunctionType
F32 = mybir.dt.float32
F32R = mybir.dt.float32r
AX_X = mybir.AxisListType.X

P = 128
S = 2048
D = 1024
KT = D // P
NT = S // P
HD = 64
BANK = 512
EPS = 1e-6
LOWEST = -3.0e38
MASKED = -1.0e32

BLK = 256
UNITS = 8


class Phase:

    def __init__(self, nc, name):
        self.nc, self.name, self.stack, self.counters = nc, name, ExitStack(), []

    def __enter__(self):
        return self

    def __exit__(self, *e):
        return self.stack.__exit__(*e)

    def sb(self, name, shape, dt=F32):
        return self.stack.enter_context(self.nc.sbuf_tensor(f"{self.name}_{name}", shape, dt))

    def banks(self, name, n):
        return self.stack.enter_context(self.nc.psum_tensor(f"{self.name}_{name}", [P, n, BANK], F32))

    def sem(self, name):
        self.counters.append(self.stack.enter_context(self.nc.semaphore(f"{self.name}_{name}")))
        return self.counters[-1]

    def sems(self, name, n):
        return [self.sem(f"{name}{i}") for i in range(n)]

    def block(self):
        self.stack.callback(self.clear)
        return self.stack.enter_context(self.nc.Block())

    def clear(self):
        for counter in self.counters:
            self.nc.gpsimd.sem_clear(counter)


def column(v):
    return v.rearrange("(n one) -> n one", one=1)


def row_on_all(v, n):
    return v.partition_broadcast(n)


def over_blocks(eng, segments, body):
    for first, turns, kinds in segments:
        if turns > 1:
            with eng.Fori(0, turns) as i:
                for j, kind in enumerate(kinds):
                    body(first + len(kinds) * i + j, i, j, kind)
        else:
            for j, kind in enumerate(kinds):
                body(first + j, 0, j, kind)


def constants(nc, ph):
    ident = ph.sb("ident", [P, P])
    ones = ph.sb("ones", [P, P])
    heads2 = ph.sb("heads2", [P, P])
    eps = ph.sb("eps", [P, 1])
    return {"ident": ident, "ones": ones, "heads2": heads2, "eps": eps}


def fill_constants(nc, c):
    with Phase(nc, "c") as ph:
        filled = ph.sem("filled")
        block = ph.block()

        @block.gpsimd
        def _(pool):
            pool.memset(c["ident"][:, :], 0.0).then_inc(filled, 1)
            pool.memset(c["ones"][:, :], 1.0).then_inc(filled, 1)
            pool.memset(c["heads2"][:, :], 0.0).then_inc(filled, 1)
            pool.memset(c["eps"][:, :], EPS).then_inc(filled, 1)
            pool.wait_ge(filled, 4)
            pool.affine_select(out=c["ident"][:, :], in_=c["ident"][:, :], compare_op=ALU.not_equal, fill=1.0,
                               base=0, pattern=[[-1, P]], channel_multiplier=1).then_inc(filled, 1)
            pool.wait_ge(filled, 5)
            pool.memset(c["heads2"][0:HD, 0:HD], 1.0).then_inc(filled, 1)
            pool.wait_ge(filled, 6)
            pool.memset(c["heads2"][HD:P, HD:P], 1.0).then_inc(filled, 1)
            pool.wait_ge(filled, 7)


def projection(nc, name, c, x, gain, w, segments, cols, rows, qk=None):
    nb = w.shape[1] // BLK
    x_t = x.rearrange("(t p) d -> t p d", p=P)
    w_b = w.rearrange("(kt p) (b n) -> b p kt n", p=P, n=BLK)
    rows_b = rows.rearrange("(k two p) (b n) -> b k p two n", two=2, p=P, n=BLK)

    with Phase(nc, name) as ph:
        ident, heads2, eps = c["ident"], c["heads2"], c["eps"]
        xt = ph.sb("xt", [P, 2, D])
        gain_all = ph.sb("gain_all", [P, D])
        stat = ph.sb("stat", [P, 2, 4])
        h_hi = ph.sb("h_hi", [P, KT, S], F32R)
        h_lo = ph.sb("h_lo", [P, KT, S], F32R)
        w_raw = ph.sb("w_raw", [P, 2, KT, BLK])
        w_hi = ph.sb("w_hi", [P, 2, KT, BLK], F32R)
        w_lo = ph.sb("w_lo", [P, 2, KT, BLK], F32R)
        stage = ph.sb("stage", [P, 4, BANK])
        squares = ph.sb("squares", [P, 2, BANK])
        root = ph.sb("root", [P, 2, BANK])
        g_raw = ph.sb("g_raw", [P, 4])
        g_tab = ph.sb("g_tab", [P, 16])
        g_now = ph.sb("g_now", [P, 2, 2])
        acc = ph.banks("acc", 4)
        aux = ph.banks("aux", 4)

        x_loaded = ph.sems("x_loaded", 4)
        gain_loaded = ph.sem("gain_loaded")
        squared = ph.sem("squared")
        rooted = ph.sem("rooted")
        inverted = ph.sem("inverted")
        normed = ph.sem("normed")
        turned = ph.sem("turned")
        hi_kept = ph.sem("hi_kept")
        lo_kept = ph.sem("lo_kept")
        w_loaded = ph.sems("w_loaded", 2)
        w_hi_made = ph.sem("w_hi_made")
        w_lo_made = ph.sem("w_lo_made")
        acc_full = ph.sem("acc_full")
        staged = ph.sems("staged", 4)
        stored = ph.sems("stored", 4)
        sq_made = ph.sem("sq_made")
        sq_summed = ph.sems("sq_summed", 2)
        root_made = ph.sems("root_made", 2)
        root_inverted = ph.sem("root_inverted")
        tab_made = ph.sem("tab_made")
        g_picked = ph.sem("g_picked")
        block = ph.block()

        def before(b, k):
            return 2 * b + k // 4

        x_slots = [xt[:, 0], xt[:, 1]] + [stage[:, n:n + 2].rearrange("p a b -> p (a b)") for n in (0, 2)]

        @block.sync
        def _(sp):
            def load_w(b, j):
                sp.dma_start(w_raw[:, j % 2], w_b[b]).then_inc(w_loaded[j % 2], 16)

            sp.dma_start(x_slots[0], x_t[0]).then_inc(x_loaded[0], 16)
            sp.dma_start(gain_all[:, :], row_on_all(gain, P)).then_inc(gain_loaded, 16)
            sp.dma_start(x_slots[1], x_t[1]).then_inc(x_loaded[1], 16)
            load_w(0, 0)
            load_w(1, 1)
            if qk is not None:
                for n, g in enumerate(qk):
                    for half in range(2):
                        sp.dma_start(g_raw[half * HD:(half + 1) * HD, n:n + 1], column(g),
                                     allow_slow_non_contiguous=True).then_inc(gain_loaded, 16)
            for t in range(2, NT):
                if t >= 4:
                    sp.wait_ge(turned, t - 3)
                sp.dma_start(x_slots[t % 4], x_t[t]).then_inc(x_loaded[t % 4], 16)

            def body(b, i, j, kind):
                if not (isinstance(b, int) and b + 2 >= nb):
                    sp.wait_ge(w_hi_made, b + 1)
                    sp.wait_ge(w_lo_made, b + 1)
                    load_w(b + 2, j)
                for k in range(UNITS):
                    sp.wait_ge(staged[k % 4], before(b, k) + 1)
                    if kind in ("rows", "silu_rows"):
                        out = rows_b[b][k]
                        src = stage[:, k % 4].rearrange("p (two n) -> p two n", two=2)
                    else:
                        out = cols[2 * b + k // 4][:, (k % 4) * BANK:(k % 4 + 1) * BANK]
                        src = stage[:, k % 4]
                    sp.dma_start(out, src).then_inc(stored[k % 4], 16)

            over_blocks(sp, segments, body)
            for k in range(4):
                sp.wait_ge(stored[k], 16 * 2 * nb)

        @block.gpsimd
        def _(pool):
            def body(b, i, j, kind):
                pool.wait_ge(w_loaded[j % 2], 16 * (b // 2 + 1) if isinstance(b, int)
                             else 16 * (len(segments[0][2]) // 2 * i + j // 2 + 1 + segments[0][0] // 2))
                pool.wait_ge(w_hi_made, b + 1)
                pool.tensor_tensor(w_lo[:, j % 2], w_raw[:, j % 2], w_hi[:, j % 2].bitcast(F32),
                                   ALU.subtract).then_inc(w_lo_made, 1)

            over_blocks(pool, segments, body)

        @block.scalar
        def _(act):
            def square(t):
                act.wait_ge(x_loaded[t % 4], 16 * (t // 4 + 1))
                if t >= 2:
                    act.wait_ge(inverted, t - 1)
                act.activation(aux[:, 2:4].rearrange("p a b -> p (a b)"), x_slots[t % 4], ACT.Square,
                               accum_out=stat[:, t % 2, 0:1]).then_inc(squared, 1)
                act.wait_ge(squared, t + 1)
                act.activation(stat[:, t % 2, 1:2], stat[:, t % 2, 0:1], ACT.Sqrt, bias=eps[:, 0:1],
                               scale=1.0 / D).then_inc(rooted, 1)

            def make_hi(b, j, loaded):
                act.wait_ge(w_loaded[j % 2], loaded)
                act.activation(w_hi[:, j % 2], w_raw[:, j % 2], ACT.Copy).then_inc(w_hi_made, 1)

            square(0)
            for t in range(NT):
                if t == 4:
                    make_hi(0, 0, 16)
                if t + 1 < NT:
                    square(t + 1)
                act.wait_ge(turned, t + 1)
                act.activation(h_hi[:, :, t * P:(t + 1) * P],
                               acc[:, 2 * (t % 2):2 * (t % 2) + 2].rearrange("p a (b n) -> p (a b) n", n=P),
                               ACT.Copy).then_inc(hi_kept, 1)

            def body(b, i, j, kind):
                if not (isinstance(b, int) and b + 1 >= nb):
                    act.wait_ge(acc_full, UNITS * b)
                    if isinstance(b, int):
                        make_hi(b + 1, j + 1, 16 * ((b + 1) // 2 + 1))
                    else:
                        first, _, kinds = segments[0]
                        make_hi(b + 1, j + 1, 16 * (len(kinds) // 2 * i + (first + j + 1) // 2 + 1))
                qb = 4 * i + j

                def sqrt(k):
                    act.wait_ge(sq_summed[k % 2], 4 * qb + k // 2 + 1)
                    act.wait_ge(staged[(k + 2) % 4], before(b, k - 2) + 1)
                    act.activation(root[:, k % 2], aux[:, k % 2], ACT.Sqrt, bias=eps[:, 0:1],
                                   scale=1.0 / HD).then_inc(root_made[k % 2], 1)

                for k in range(UNITS):
                    if kind == "head_norm":
                        act.wait_ge(acc_full, UNITS * b + k + 1)
                        act.wait_ge(sq_summed[k % 2], 4 * qb + k // 2)
                        act.activation(squares[:, k % 2], acc[:, k % 4], ACT.Square).then_inc(sq_made, 1)
                        if k >= 1:
                            sqrt(k - 1)
                    elif kind in ("silu_rows", "silu_cols"):
                        act.wait_ge(acc_full, UNITS * b + k + 1)
                        act.wait_ge(stored[k % 4], 16 * before(b, k))
                        act.activation(stage[:, k % 4], acc[:, k % 4], ACT.Silu).then_inc(staged[k % 4], 1)
                if kind == "head_norm":
                    sqrt(UNITS - 1)

            over_blocks(act, segments, body)

        @block.vector
        def _(dve):
            dve.wait_ge(gain_loaded, 16 * (1 + (8 if qk is not None else 0)))
            if qk is not None:
                for half in range(2):
                    at = slice(half * HD, (half + 1) * HD)
                    for ct in range(4):
                        diff = 2.0 ** (2 * (ct + 1)) / 8
                        dil = 2.0 ** (2 * ct + half + 1) / 8
                        for n, factor in enumerate((diff, 1.0, dil, 1.0)):
                            dve.tensor_scalar(g_tab[at, 4 * n + ct:4 * n + ct + 1], g_raw[at, n:n + 1], factor,
                                              None, ALU.mult).then_inc(tab_made, 1)
                dve.wait_ge(tab_made, 32)
            def norm(t):
                dve.wait_ge(rooted, t + 1)
                dve.reciprocal(stat[:, t % 2, 2:3], stat[:, t % 2, 1:2]).then_inc(inverted, 1)
                dve.wait_ge(inverted, t + 1)
                dve.wait_ge(x_loaded[t % 4], 16 * (t // 4 + 1))
                dve.scalar_tensor_tensor(out=x_slots[t % 4], in0=x_slots[t % 4], scalar=stat[:, t % 2, 2:3],
                                         in1=gain_all[:, :], op0=ALU.mult, op1=ALU.mult).then_inc(normed, 1)

            norm(0)
            for t in range(NT):
                if t + 1 < NT:
                    norm(t + 1)
                dve.wait_ge(hi_kept, t + 1)
                at = slice(t * P, (t + 1) * P)
                dve.tensor_tensor(h_lo[:, :, at],
                                  acc[:, 2 * (t % 2):2 * (t % 2) + 2].rearrange("p a (b n) -> p (a b) n", n=P),
                                  h_hi[:, :, at].bitcast(F32), ALU.subtract).then_inc(lo_kept, 1)

            def body(b, i, j, kind):
                qb = 4 * i + j
                if kind == "head_norm":
                    dve.wait_ge(staged[3], 2 * b)
                    dve.tensor_copy(g_now[:, j % 2], g_tab[:, :].rearrange("p (q two) -> p q two", two=2)[:, qb])\
                       .then_inc(g_picked, 1)
                    dve.wait_ge(g_picked, qb + 1)
                for k in range(UNITS):
                    if kind == "head_norm":
                        dve.wait_ge(root_made[k % 2], 4 * qb + k // 2 + 1)
                        dve.reciprocal(root[:, k % 2], root[:, k % 2]).then_inc(root_inverted, 1)
                        dve.wait_ge(root_inverted, UNITS * qb + k + 1)
                        dve.wait_ge(stored[k % 4], 16 * before(b, k))
                        dve.scalar_tensor_tensor(out=stage[:, k % 4], in0=acc[:, k % 4],
                                                 scalar=g_now[:, j % 2, k // 4:k // 4 + 1], in1=root[:, k % 2],
                                                 op0=ALU.mult, op1=ALU.mult).then_inc(staged[k % 4], 1)
                    elif kind in ("rows", "cols", "cols_scaled"):
                        dve.wait_ge(acc_full, UNITS * b + k + 1)
                        dve.wait_ge(stored[k % 4], 16 * before(b, k))
                        factor = HD ** -0.5 if kind == "cols_scaled" else 1.0
                        dve.tensor_scalar(stage[:, k % 4], acc[:, k % 4], factor, None, ALU.mult)\
                           .then_inc(staged[k % 4], 1)

            over_blocks(dve, segments, body)

        @block.tensor
        def _(pe):
            for t in range(NT):
                pe.wait_ge(normed, t + 1)
                if t >= 2:
                    pe.wait_ge(lo_kept, t - 1)
                for kt in range(KT):
                    mm = pe.transpose(acc[:, 2 * (t % 2) + kt // 4, (kt % 4) * P:(kt % 4 + 1) * P],
                                      x_slots[t % 4][:, kt * P:(kt + 1) * P], ident[:, :])
                mm.then_inc(turned, 1)
            pe.wait_ge(lo_kept, NT)

            def body(b, i, j, kind):
                pe.wait_ge(w_hi_made, b + 1)
                pe.wait_ge(w_lo_made, b + 1)
                qb = 4 * i + j

                def sum_squares(k):
                    pe.wait_ge(sq_made, UNITS * qb + k + 1)
                    pe.wait_ge(root_made[k % 2], 4 * qb + k // 2)
                    pe.matmul(aux[:, k % 2], heads2[:, :], squares[:, k % 2], start=True, stop=True)\
                      .then_inc(sq_summed[k % 2], 1)

                for k in range(UNITS):
                    pe.wait_ge(staged[k % 4], before(b, k))
                    if kind in ("rows", "silu_rows"):
                        for two in range(2):
                            at = slice((2 * k + two) * P, (2 * k + two + 1) * P)
                            for kt in range(KT):
                                for n, (h_part, w_part) in enumerate(((h_hi, w_hi), (h_hi, w_lo), (h_lo, w_hi))):
                                    mm = pe.matmul(acc[:, k % 4, two * BLK:(two + 1) * BLK],
                                                   h_part[:, kt, at], w_part[:, j % 2, kt],
                                                   start=(kt == 0 and n == 0), stop=(kt == KT - 1 and n == 2))
                    else:
                        ct, tc = k // 4, k % 4
                        for kt in range(KT):
                            for n, (w_part, h_part) in enumerate(((w_hi, h_hi), (w_hi, h_lo), (w_lo, h_hi))):
                                mm = pe.matmul(acc[:, k % 4], w_part[:, j % 2, kt, ct * P:(ct + 1) * P],
                                               h_part[:, kt, tc * BANK:(tc + 1) * BANK],
                                               start=(kt == 0 and n == 0), stop=(kt == KT - 1 and n == 2))
                    mm.then_inc(acc_full, 1)
                    if kind == "head_norm" and k >= 1:
                        sum_squares(k - 1)
                if kind == "head_norm":
                    sum_squares(UNITS - 1)

            over_blocks(pe, segments, body)


IN_SEGMENTS = [(0, 2, ["head_norm"] * 4 + ["rows"] * 2), (12, 1, ["silu_cols"] * 2 + ["silu_rows"] * 2)]
SWA_SEGMENTS = [(0, 2, ["cols_scaled"] * 2), (4, 1, ["cols", "rows"] + ["silu_cols"] * 4)]

DQ, DK, DV, BQ, BK, BV, ZA, ZB = (4 * n for n in range(8))
DIFF_HEADS = 4
DIL_HEADS = 8
LAM_INIT = 0.2


def diff_attention(nc, c, lambdas, cols, rows, a_t, ss_t):
    VW = 2 * HD
    QUAD = 4 * P
    SPAN = 2 * S - P
    HALF = S // 2
    TPI = 2 * NT
    PAIRS = TPI // 2

    with Phase(nc, "d") as ph:
        ident, ones = c["ident"], c["ones"]
        k_raw = ph.sb("k_raw", [P, S])
        k_hi = ph.sb("k_hi", [P, 2, 2, S], F32R)
        k_lo = ph.sb("k_lo", [P, 2, 2, S], F32R)
        v = ph.sb("v", [P, 2, NT, VW])
        q_raw = ph.sb("q_raw", [P, 2, 2, QUAD])
        q_parts = ph.sb("q_parts", [P, 2, 2, P], F32R)
        dist = ph.sb("dist", [P, SPAN])
        e = ph.sb("e", [P, 3, 2, S])
        w_t = ph.sb("w_t", [P, 2, NT, 2 * P])
        slope = ph.sb("slope", [P, 2])
        top = ph.sb("top", [P, 2, 2, 2])
        neg_top = ph.sb("neg_top", [P, 2, 2])
        total = ph.sb("total", [P, 2, 2])
        ratio = ph.sb("ratio", [P, 2, 4])
        l_sq = ph.sb("l_sq", [P, 4, 2, P])
        a_out = ph.sb("a_out", [P, 2, 2 * P])
        a_sq = ph.sb("a_sq", [P, 2, 2 * P])
        ss_out = ph.sb("ss_out", [P, 2, 2 * P])
        lam_in = ph.sb("lam_in", [P, 4, HD])
        lam = ph.sb("lam", [P, 8])
        score = ph.banks("score", 4)
        turn = ph.banks("turn", 2)
        out = ph.banks("out", 2)
        av, ss = out[:, :, 0:2 * P], out[:, :, 2 * P:4 * P]

        lam_loaded = ph.sem("lam_loaded")
        passed = ph.sem("passed")
        lam_step = ph.sem("lam_step")
        lam_exped = ph.sem("lam_exped")
        counted = ph.sem("counted")
        dist_made = ph.sem("dist_made")
        slope_set = ph.sem("slope_set")
        k_loaded = ph.sem("k_loaded")
        early_loaded = ph.sem("early_loaded")
        v_loaded = ph.sems("v_loaded", 2)
        q_loaded = ph.sems("q_loaded", 2)
        k_hi_made = ph.sem("k_hi_made")
        k_made = ph.sem("k_made")
        q_hi_made = ph.sem("q_hi_made")
        q_made = ph.sem("q_made")
        scored = ph.sem("scored")
        score_read = ph.sems("score_read", 2)
        top_made = ph.sem("top_made")
        exped = ph.sem("exped")
        ratio_step = ph.sem("ratio_step")
        squared_l = ph.sem("squared_l")
        mixed = ph.sem("mixed")
        turned = ph.sem("turned")
        moved_act = ph.sem("moved_act")
        moved_dve = ph.sem("moved_dve")
        av_done = ph.sems("av_done", 2)
        a_moved = ph.sems("a_moved", 2)
        a_stored = ph.sems("a_stored", 2)
        a_squared = ph.sem("a_squared")
        ss_done = ph.sems("ss_done", 2)
        ss_moved = ph.sems("ss_moved", 2)
        ss_stored = ph.sems("ss_stored", 2)
        block = ph.block()
        early = e[:, 2, 1]

        @block.sync
        def _(sp):
            def load_k(h, s, to=k_raw, arrived=k_loaded):
                if h >= 1:
                    sp.wait_ge(k_made, 2 * h + s)
                row = s * HD
                for half in range(2):
                    sp.dma_start(to[half * HD:(half + 1) * HD, :], cols[DK + h][row:row + HD, :])\
                      .then_inc(arrived, 16)

            def load_v(h):
                if h >= 2:
                    sp.wait_ge(av_done[1], (h - 1) * NT // 4)
                    sp.wait_ge(av_done[0], (h - 1) * NT // 4)
                at = (DV + h) * P
                sp.dma_start(v[:, h % 2], rows[:, at:at + VW].rearrange("(t p) n -> p t n", p=P))\
                  .then_inc(v_loaded[h % 2], 16)

            def load_q(h, quad):
                n = 4 * h + quad
                if n >= 2:
                    sp.wait_ge(q_made, 4 * (n - 1))
                for half in range(2):
                    sp.dma_start(q_raw[half * HD:(half + 1) * HD, n % 2],
                                 cols[DQ + h][:, quad * QUAD:(quad + 1) * QUAD].rearrange("(s e) t -> e s t", s=2))\
                      .then_inc(q_loaded[n % 2], 16)

            def store(pair):
                h, at = pair // 8, (pair % 8) * 2 * P
                s = pair % 2
                sp.wait_ge(a_moved[s], pair // 2 + 1)
                sp.dma_start(a_t[h][:, at:at + 2 * P], a_out[:, s]).then_inc(a_stored[s], 16)
                sp.wait_ge(ss_moved[s], pair // 2 + 1)
                sp.dma_start(ss_t[h][:, at:at + 2 * P], ss_out[:, s]).then_inc(ss_stored[s], 16)

            load_k(0, 0)
            load_q(0, 0)
            load_k(0, 1, early, early_loaded)
            for n, vec in enumerate(lambdas):
                sp.dma_start(lam_in[:, n], row_on_all(vec, P)).then_inc(lam_loaded, 16)
            load_q(0, 1)
            load_v(0)
            for h in range(DIFF_HEADS):
                for quad in range(4):
                    nxt = 4 * h + quad + 2
                    if nxt < 4 * DIFF_HEADS:
                        load_q(nxt // 4, nxt % 4)
                    if quad == 0 and h + 1 < DIFF_HEADS:
                        load_v(h + 1)
                    if quad in (1, 2) and h + 1 < DIFF_HEADS:
                        load_k(h + 1, quad - 1)
                    for pair in (8 * h + 2 * quad - 1, 8 * h + 2 * quad):
                        if pair >= 0:
                            store(pair)
            store(8 * DIFF_HEADS - 1)
            for s in range(2):
                sp.wait_ge(a_stored[s], 16 * 4 * DIFF_HEADS)
                sp.wait_ge(ss_stored[s], 16 * 4 * DIFF_HEADS)

        @block.gpsimd
        def _(pool):
            pool.iota(e[:, :, :, :].rearrange("p a b n -> p (a b n)")[:, 0:SPAN], pattern=[[-1, SPAN]],
                      base=S - P, channel_multiplier=1, allow_small_or_imprecise_dtypes=True).then_inc(counted, 1)
            for h in range(1, DIFF_HEADS):
                for s in range(2):
                    pool.wait_ge(k_loaded, 32 * (2 * h + s))
                    if h >= 2:
                        pool.wait_ge(scored, 4 * NT * (h - 1))
                    pool.tensor_copy(k_hi[:, h % 2, s], k_raw[:, :]).then_inc(k_hi_made, 1)
                    pool.wait_ge(k_hi_made, 2 * h + s + 1)
                    pool.tensor_tensor(k_lo[:, h % 2, s], k_raw[:, :], k_hi[:, h % 2, s].bitcast(F32),
                                       ALU.subtract).then_inc(k_made, 1)

        @block.scalar
        def _(act):
            for s in range(2):
                act.wait_ge((k_loaded, early_loaded)[s], 32)
                act.activation(k_hi[:, 0, s], (k_raw[:, :], early)[s], ACT.Copy).then_inc(k_hi_made, 1)
            act.wait_ge(lam_step, 2)
            act.activation(lam[:, 2:4], lam[:, 0:2], ACT.Exp).then_inc(lam_exped, 1)

            with act.Fori(0, 2) as i:
                def split_q(m):
                    n = TPI * i + m
                    act.wait_ge(q_loaded[(m // 4) % 2], 32 * (TPI // 8 * i + m // 8 + 1))
                    act.wait_ge(scored, 4 * TPI * i + 4 * max(m - 1, 0))
                    act.activation(q_parts[:, m % 2], q_raw[:, (m // 4) % 2, :, (m % 4) * P:(m % 4 + 1) * P],
                                   ACT.Copy).then_inc(q_hi_made, 1)

                def exp(m, s):
                    n = TPI * i + m
                    act.wait_ge(top_made, 2 * n + s + 1)
                    act.activation(e[:, m % 3, s], e[:, m % 3, s], ACT.Exp, bias=neg_top[:, m % 2, s:s + 1],
                                   accum_out=total[:, m % 2, s:s + 1]).then_inc(exped, 1)

                def move(m, r):
                    n = TPI * i + m
                    pair = m // 2
                    act.wait_ge(turned, 4 * n + r + 1)
                    act.wait_ge(av_done[pair % 2], PAIRS // 2 * i + pair // 2)
                    act.activation(w_t[:, pair % 2, 4 * r:4 * r + 4, (m % 2) * P:(m % 2 + 1) * P],
                                   turn[:, r % 2].rearrange("p (b n) -> p b n", n=P), ACT.Copy)\
                       .then_inc(moved_act, 1)

                def square(pair):
                    act.wait_ge(av_done[pair % 2], PAIRS // 2 * i + pair // 2 + 1)
                    act.wait_ge(ss_done[pair % 2], PAIRS // 2 * i + pair // 2)
                    act.activation(a_sq[:, pair % 2], av[:, pair % 2],
                                   ACT.Square).then_inc(a_squared, 1)

                def move_a(pair):
                    act.wait_ge(a_stored[pair % 2], 16 * (PAIRS // 2 * i + pair // 2))
                    act.activation(a_out[:, pair % 2], av[:, pair % 2], ACT.Copy).then_inc(a_moved[pair % 2], 1)

                def move_ss(pair):
                    act.wait_ge(ss_done[pair % 2], PAIRS // 2 * i + pair // 2 + 1)
                    act.wait_ge(ss_stored[pair % 2], 16 * (PAIRS // 2 * i + pair // 2))
                    act.activation(ss_out[:, pair % 2], ss[:, pair % 2],
                                   ACT.Copy).then_inc(ss_moved[pair % 2], 1)

                for m in range(-3, TPI):
                    if m >= 0:
                        move(m, 0)
                    if 0 <= m + 2 < TPI:
                        exp(m + 2, 0)
                    if m >= 4 and m % 2 == 0:
                        square(m // 2 - 2)
                        move_a(m // 2 - 2)
                    if m + 3 < TPI:
                        split_q(m + 3)
                    if m >= 0:
                        move(m, 2)
                        move(m, 3)
                    if 0 <= m + 2 < TPI:
                        exp(m + 2, 1)
                    if m >= 4 and m % 2 == 0:
                        move_ss(m // 2 - 2)
                for pair in (PAIRS - 2, PAIRS - 1):
                    square(pair)
                    move_a(pair)
                    move_ss(pair)

        @block.vector
        def _(dve):
            for s in range(2):
                dve.wait_ge(k_hi_made, s + 1)
                dve.tensor_tensor(k_lo[:, 0, s], (k_raw[:, :], early)[s], k_hi[:, 0, s].bitcast(F32), ALU.subtract)\
                   .then_inc(k_made, 1)
            dve.wait_ge(counted, 1)
            counts = e[:, :, :, :].rearrange("p a b n -> p (a b n)")[:, 0:SPAN]
            dve.scalar_tensor_tensor(out=dist[:, :], in0=counts, scalar=-1.0, in1=counts, op0=ALU.mult,
                                     op1=ALU.min).then_inc(dist_made, 1)
            dve.wait_ge(lam_loaded, 64)
            for n in range(2):
                dve.tensor_tensor_reduce(lam_in[:, 2 * n], lam_in[:, 2 * n], lam_in[:, 2 * n + 1], 1.0, 0.0,
                                         ALU.mult, ALU.add, lam[:, n:n + 1]).then_inc(lam_step, 1)
            dve.wait_ge(lam_exped, 1)
            dve.tensor_tensor(lam[:, 4:5], lam[:, 3:4], lam[:, 2:3], ALU.subtract).then_inc(lam_step, 1)
            dve.wait_ge(lam_step, 3)
            dve.tensor_scalar(lam[:, 5:6], lam[:, 4:5], -LAM_INIT, None, ALU.add).then_inc(lam_step, 1)
            for n in range(2):
                dve.memset(slope[:, n:n + 1], 2.0 ** (-2 * (n + 1))).then_inc(slope_set, 1)
            dve.wait_ge(lam_step, 4)
            dve.wait_ge(dist_made, 1)
            dve.wait_ge(slope_set, 2)

            with dve.Fori(0, 2) as i:
                def split_q(m):
                    n = TPI * i + m
                    dve.wait_ge(q_hi_made, n + 1)
                    dve.tensor_tensor(q_parts[HD:P, m % 2], q_raw[HD:P, (m // 4) % 2, :, (m % 4) * P:(m % 4 + 1) * P],
                                      q_parts[HD:P, m % 2].bitcast(F32), ALU.subtract).then_inc(q_made, 1)

                def bias_and_top(m, s):
                    n, t = TPI * i + m, m % NT
                    for half in range(2):
                        dve.wait_ge(turned, 4 * TPI * i + max(4 * (m - 2), 0))
                        dve.wait_ge(exped, 2 * TPI * i + max(2 * (m - 1), 0))
                        dve.wait_ge(scored, 4 * n + 2 * s + half + 1)
                        dve.sem_inc(passed, 1)
                        at = S - P - t * P + half * HALF
                        dve.tensor_tensor_reduce(
                            e[:, m % 3, s, half * HALF:(half + 1) * HALF],
                            score[:, 2 * half:2 * half + 2].rearrange("p a b -> p (a b)"),
                            dist[:, at:at + HALF], slope[:, m // NT:m // NT + 1], LOWEST, ALU.add, ALU.max,
                            top[:, m % 2, s, half:half + 1]).then_inc(score_read[half], 1)

                def negate_top(m, s):
                    n = TPI * i + m
                    for half in range(2):
                        dve.wait_ge(score_read[half], 2 * n + s + 1)
                    dve.tensor_reduce(neg_top[:, m % 2, s:s + 1], top[:, m % 2, s], AX_X, ALU.max,
                                      negate=True).then_inc(top_made, 1)

                def invert_total(m):
                    n = TPI * i + m
                    dve.wait_ge(exped, 2 * n + 2)
                    l0, l1 = total[:, m % 2, 0:1], total[:, m % 2, 1:2]
                    dve.reciprocal(ratio[:, m % 2, 0:1], l1).then_inc(ratio_step, 1)
                    dve.tensor_scalar(ratio[:, m % 2, 2:3], l0, l0, 2 * HD * EPS, ALU.mult, ALU.mult)\
                       .then_inc(squared_l, 1)

                def weigh(m):
                    n = TPI * i + m
                    pair = m // 2
                    dve.wait_ge(ratio_step, 2 * n + 1)
                    dve.tensor_scalar(ratio[:, m % 2, 1:2], total[:, m % 2, 0:1], ratio[:, m % 2, 0:1], lam[:, 5:6],
                                      ALU.mult, ALU.mult).then_inc(ratio_step, 1)
                    dve.wait_ge(squared_l, 2 * n + 1)
                    dve.wait_ge(ss_done[pair % 2], PAIRS // 2 * i + max(pair // 2 - 1, 0))
                    dve.tensor_scalar(l_sq[:, pair % 4, m % 2], ones[:, :], ratio[:, m % 2, 2:3], None, ALU.mult)\
                       .then_inc(squared_l, 1)

                def mix(m):
                    n = TPI * i + m
                    dve.wait_ge(ratio_step, 2 * n + 2)
                    dve.scalar_tensor_tensor(out=e[:, m % 3, 0], in0=e[:, m % 3, 1], scalar=ratio[:, m % 2, 1:2],
                                             in1=e[:, m % 3, 0], op0=ALU.mult, op1=ALU.add).then_inc(mixed, 1)

                def move(m, r):
                    n = TPI * i + m
                    pair = m // 2
                    dve.wait_ge(turned, 4 * n + r + 1)
                    dve.wait_ge(av_done[pair % 2], PAIRS // 2 * i + pair // 2)
                    dve.tensor_copy(w_t[:, pair % 2, 4 * r:4 * r + 4, (m % 2) * P:(m % 2 + 1) * P],
                                    turn[:, r % 2].rearrange("p (b n) -> p b n", n=P)).then_inc(moved_dve, 1)

                for m in range(-3, TPI):
                    if 0 <= m + 1 < TPI:
                        invert_total(m + 1)
                    if 0 <= m + 2 < TPI:
                        bias_and_top(m + 2, 0)
                    if 0 <= m + 1 < TPI:
                        weigh(m + 1)
                    if 0 <= m + 2 < TPI:
                        negate_top(m + 2, 0)
                    if m >= 0:
                        move(m, 1)
                    if 0 <= m + 2 < TPI:
                        bias_and_top(m + 2, 1)
                    if m + 3 < TPI:
                        split_q(m + 3)
                    if 0 <= m + 2 < TPI:
                        negate_top(m + 2, 1)
                    if 0 <= m + 1 < TPI:
                        mix(m + 1)
                for n in range(2):
                    dve.tensor_scalar(slope[:, n:n + 1], slope[:, n:n + 1], 2.0 ** -4, None, ALU.mult)\
                       .then_inc(slope_set, 1)
                dve.wait_ge(slope_set, 2 * i + 4)

        @block.tensor
        def _(pe):
            with pe.Fori(0, 2) as i:
                def scores(m, s, half):
                    n, par = TPI * i + m, m // NT
                    if half == 0:
                        pe.wait_ge(q_made, n + 1)
                    if m % NT == 0 and half == 0:
                        pe.wait_ge(k_made, 4 * i + 2 * par + s + 1)
                    pe.wait_ge(score_read[half], 2 * n + s)
                    for b in range(2):
                        at = half * HALF + b * BANK
                        pe.matmul(score[:, 2 * half + b], q_parts[:, m % 2, s], k_hi[:, par, s, at:at + BANK],
                                  start=True, stop=False)
                        mm = pe.matmul(score[:, 2 * half + b], q_parts[:, m % 2, s],
                                       k_lo[:, par, s, at:at + BANK], start=False, stop=True)
                    mm.then_inc(scored, 1)

                def transposes(m, r):
                    n = TPI * i + m
                    if r == 0:
                        pe.wait_ge(mixed, n + 1)
                    if r == 3:
                        pe.wait_ge(moved_dve, n + 1)
                    else:
                        pe.wait_ge(moved_act, 3 * n + r // 2)
                    for b in range(4):
                        mm = pe.transpose(turn[:, r % 2, b * P:(b + 1) * P],
                                          e[:, m % 3, 0, (4 * r + b) * P:(4 * r + b + 1) * P], ident[:, :])
                    mm.then_inc(turned, 1)

                def weigh_values(pair, first, last):
                    n, par = TPI * i + 2 * pair + 1, pair // 8
                    if first == 0:
                        if pair % 8 == 0:
                            pe.wait_ge(v_loaded[par], 16 * (i + 1))
                        pe.wait_ge(moved_act, 3 * n + 3)
                        pe.wait_ge(moved_dve, n + 1)
                        pe.wait_ge(ss_moved[pair % 2], PAIRS // 2 * i + pair // 2)
                    for kt in range(first, last):
                        mm = pe.matmul(av[:, pair % 2], v[:, par, kt],
                                       w_t[:, pair % 2, kt], start=(kt == 0), stop=(kt == NT - 1))
                    if last == NT:
                        mm.then_inc(av_done[pair % 2], 1)

                def sum_squares(pair):
                    n = TPI * i + 2 * pair + 1
                    pe.wait_ge(a_squared, PAIRS * i + pair + 1)
                    pe.wait_ge(a_moved[pair % 2], PAIRS // 2 * i + pair // 2 + 1)
                    pe.wait_ge(squared_l, 2 * n + 2)
                    pe.wait_ge(ss_moved[pair % 2], PAIRS // 2 * i + pair // 2)
                    for b in range(2):
                        half = slice(b * P, (b + 1) * P)
                        pe.matmul(ss[:, pair % 2, half], ones[:, :], a_sq[:, pair % 2, b * P:(b + 1) * P],
                                  start=True, stop=False)
                        mm = pe.matmul(ss[:, pair % 2, half], l_sq[:, pair % 4, b], ident[:, :], start=False, stop=True)
                    mm.then_inc(ss_done[pair % 2], 1)

                for m in range(-2, TPI):
                    kt = NT // 2 * (m % 2)

                    def values(n, upto):
                        if m >= 2:
                            weigh_values(m // 2 - 1, kt + n, kt + upto)

                    if m + 2 < TPI:
                        scores(m + 2, 0, 0)
                        scores(m + 2, 0, 1)
                    if m >= 0:
                        transposes(m, 0)
                        transposes(m, 1)
                    values(0, 2)
                    if m + 2 < TPI:
                        scores(m + 2, 1, 0)
                        scores(m + 2, 1, 1)
                    if m >= 0:
                        transposes(m, 2)
                        transposes(m, 3)
                    values(2, 8)
                    if m >= 4 and m % 2 == 0:
                        sum_squares(m // 2 - 2)
                sum_squares(PAIRS - 2)
                weigh_values(PAIRS - 1, 0, NT)
                sum_squares(PAIRS - 1)

DILATIONS = (1, 4, 16)
REACH = 64
PAIR_OUT = 2 * HD + 4


def dilated_units():
    chunk = 0
    for d in DILATIONS:
        tiles = NT // d
        for cls in range(d):
            for b in range(tiles):
                yield d, cls, b, chunk + b
            chunk += tiles + 1 if tiles > 1 else 1


def dilated_attention(nc, c, cols, rows, o_parts):
    PAIRS = DIL_HEADS // 2
    UPP = 3 * NT
    UPT = 2 * UPP
    PAD = REACH * 4
    WIN = 2 * P
    CHUNKS = (NT + 1) + 4 * (NT // 4 + 1) + NT
    V_DMAS = 3 + 4 * 3 + 1
    units = list(dilated_units())

    with Phase(nc, "l") as ph:
        ident = c["ident"]
        raw = ph.sb("raw", [P, 2, S])
        q_parts = ph.sb("q_parts", [P, 2, 2, S], F32R)
        k_hi = ph.sb("k_hi", [P, 2, 2, S + 2 * PAD], F32R)
        k_lo = ph.sb("k_lo", [P, 2, 2, S + 2 * PAD], F32R)
        v = ph.sb("v", [P, 2, CHUNKS, 2 * HD])
        tables = ph.sb("tables", [P, 7, WIN])
        e = ph.sb("e", [P, 4, 2, WIN])
        e_t = ph.sb("e_t", [P, 2, 4, P])
        stage = ph.sb("stage", [P, 8, PAIR_OUT])
        top = ph.sb("top", [P, 4, 2])
        slope = ph.sb("slope", [P, 4])
        score = ph.banks("score", 4)
        turn = ph.banks("turn", 2)
        out = ph.banks("out", 2)

        raw_loaded = ph.sems("raw_loaded", 2)
        early_loaded = ph.sems("early_loaded", 2)
        v_loaded = ph.sems("v_loaded", 2)
        padded = ph.sem("padded")
        v_padded = ph.sem("v_padded")
        hi_made = ph.sem("hi_made")
        parts_made = ph.sem("parts_made")
        counted = ph.sem("counted")
        distance = ph.sem("distance")
        masked = ph.sem("masked")
        slope_set = ph.sem("slope_set")
        scored = ph.sem("scored")
        passed = ph.sem("passed")
        score_read = ph.sem("score_read")
        top_made = ph.sem("top_made")
        exped = ph.sem("exped")
        turned = ph.sem("turned")
        moved = ph.sems("moved", 2)
        valued = ph.sem("valued")
        staged = ph.sem("staged")
        stored = ph.sems("stored", 8)
        block = ph.block()
        first_raw = [raw[:, 0], raw[:, 1], q_parts[:, 1, 0].bitcast(F32), q_parts[:, 1, 1].bitcast(F32)]

        @block.sync
        def _(sp):
            def load_raw(pair, item):
                g = 4 * pair + item
                to, arrived = raw[:, g % 2], raw_loaded[g % 2]
                if pair == 0 and item >= 2:
                    to, arrived = first_raw[item], early_loaded[item - 2]
                elif pair >= 1:
                    sp.wait_ge(parts_made, g - 1)
                tile = (BQ, BK)[item // 2] + pair
                for half in range(2):
                    sp.dma_start(to[half * HD:(half + 1) * HD, :], cols[tile][(item % 2) * HD:(item % 2 + 1) * HD, :])\
                      .then_inc(arrived, 16)

            def load_v(pair):
                if pair >= 1:
                    sp.wait_ge(valued, UPP * (pair - 1))
                else:
                    sp.wait_ge(v_padded, 20)
                at = BV * P + pair * 2 * HD
                src, dst, arrived = rows[:, at:at + 2 * HD], v[:, pair % 2], v_loaded[pair % 2]
                chunk = 0
                for d in (1, 4):
                    tiles = NT // d
                    for cls in range(d):
                        own = src.rearrange("(i d) n -> d i n", d=d)[cls]
                        sp.dma_start(dst[REACH:P, chunk], own[0:REACH, :]).then_inc(arrived, 16)
                        sp.dma_start(dst[:, chunk + 1:chunk + tiles],
                                     own[REACH:REACH + (tiles - 1) * P, :].rearrange("(j p) n -> p j n", p=P))\
                          .then_inc(arrived, 16)
                        sp.dma_start(dst[0:REACH, chunk + tiles], own[tiles * P - REACH:tiles * P, :])\
                          .then_inc(arrived, 16)
                        chunk += tiles + 1
                sp.dma_start(dst[:, chunk:chunk + NT], src.rearrange("(i d) n -> i d n", d=NT)).then_inc(arrived, 16)

            for item in range(4):
                load_raw(0, item)
            load_v(0)
            for pair in range(PAIRS):
                for u, (d, cls, b, _) in enumerate(units):
                    if pair + 1 < PAIRS:
                        if u in (5, 10, 18, 26):
                            load_raw(pair + 1, (5, 10, 18, 26).index(u))
                        if u == 8:
                            load_v(pair + 1)
                    n = UPP * pair + u
                    sp.wait_ge(staged, n + 1)
                    own = o_parts[DILATIONS.index(d)][:, pair].rearrange("(i d) n -> d i n", d=d)[cls]
                    sp.dma_start(own[b * P:(b + 1) * P, :], stage[:, n % 8]).then_inc(stored[n % 8], 16)
            for s in range(8):
                sp.wait_ge(stored[s], 16 * UPP * PAIRS // 8)

        @block.gpsimd
        def _(pool):
            pool.iota(e[:, 0, 0], pattern=[[-1, WIN]], base=REACH, channel_multiplier=1,
                      allow_small_or_imprecise_dtypes=True).then_inc(counted, 1)
            for par in range(2):
                for part in (k_hi, k_lo):
                    for edge in (slice(0, PAD), slice(PAD + S, S + 2 * PAD)):
                        pool.memset(part[:, par, :, edge].bitcast(F32), 0.0).then_inc(padded, 1)

            def split(pair):
                par = pair % 2
                for item in range(4):
                    g = 4 * pair + item
                    pool.wait_ge(raw_loaded[g % 2], 32 * (g // 2))
                    if pair >= 2 and item == 0:
                        pool.wait_ge(scored, UPP * (pair - 1))
                    if pair == 1 and item == 0:
                        pool.wait_ge(padded, 8)
                    pool.wait_ge(parts_made, g)
                    h = item % 2
                    if item < 2:
                        pool.tensor_copy(q_parts[:, par, h], raw[:, g % 2]).then_inc(hi_made, 1)
                        pool.wait_ge(hi_made, g + 1)
                        pool.tensor_tensor(q_parts[HD:P, par, h], raw[HD:P, g % 2], q_parts[HD:P, par, h].bitcast(F32),
                                           ALU.subtract).then_inc(parts_made, 1)
                    else:
                        at = slice(PAD, PAD + S)
                        pool.tensor_copy(k_hi[:, par, h, at], raw[:, g % 2]).then_inc(hi_made, 1)
                        pool.wait_ge(hi_made, g + 1)
                        pool.tensor_tensor(k_lo[:, par, h, at], raw[:, g % 2], k_hi[:, par, h, at].bitcast(F32),
                                           ALU.subtract).then_inc(parts_made, 1)

            pool.wait_ge(distance, 8)
            steps = 0
            for n in range(7):
                limits = [(2 * REACH, -1, 1), (0, 1, -1)]
                if n % 3 == 1:
                    limits.append((-REACH, 1, 0))
                if n % 3 == 2:
                    limits.append((WIN - REACH - 1, -1, 0))
                for base, step, channel in limits:
                    pool.affine_select(out=tables[:, n], in_=tables[:, n], compare_op=ALU.is_ge, fill=MASKED,
                                       base=base, pattern=[[step, WIN]], channel_multiplier=channel)\
                        .then_inc(masked, 1)
                    steps += 1
                    pool.wait_ge(masked, steps)
            assert steps == 18
            for pair in range(1, PAIRS):
                split(pair)

        @block.scalar
        def _(act):
            for item in range(4):
                act.wait_ge((raw_loaded + early_loaded)[item], 32)
                if item == 2:
                    act.wait_ge(padded, 8)
                hi = q_parts[:, 0, item] if item < 2 else k_hi[:, 0, item % 2, PAD:PAD + S]
                act.activation(hi, first_raw[item], ACT.Copy).then_inc(hi_made, 1)

            with act.Fori(0, 2) as i:
                def exp(u):
                    n = UPT * i + u
                    w = WIN if units[u % UPP][0] < NT else P
                    act.wait_ge(top_made, n + 1)
                    for h in range(2):
                        act.activation(e[:, u % 4, h, 0:w], e[:, u % 4, h, 0:w], ACT.Exp,
                                       bias=stage[:, u % 8, 2 * HD + h:2 * HD + h + 1],
                                       accum_out=stage[:, u % 8, 2 * HD + 2 + h:2 * HD + 3 + h]).then_inc(exped, 1)

                def move(u):
                    n = UPT * i + u
                    w = 4 if units[u % UPP][0] < NT else 2
                    act.wait_ge(turned, n + 1)
                    act.wait_ge(valued, UPT * i + max(u - 1, 0))
                    act.activation(e_t[:, u % 2, 0:w], turn[:, u % 2, 0:w * P].rearrange("p (b n) -> p b n", n=P),
                                   ACT.Copy).then_inc(moved[u % 2], 1)

                for u in range(-3, UPT):
                    if 0 <= u + 2 < UPT:
                        exp(u + 2)
                    if 0 <= u + 1 < UPT and (u + 1) % 2 == 0:
                        move(u + 1)

        @block.vector
        def _(dve):
            chunk = 0
            for d in (1, 4):
                tiles = NT // d
                for cls in range(d):
                    for par in range(2):
                        dve.memset(v[0:REACH, par, chunk], 0.0).then_inc(v_padded, 1)
                        dve.memset(v[REACH:P, par, chunk + tiles], 0.0).then_inc(v_padded, 1)
                    chunk += tiles + 1
            dve.wait_ge(counted, 1)
            dve.scalar_tensor_tensor(out=e[:, 1, 0], in0=e[:, 0, 0], scalar=-1.0, in1=e[:, 0, 0], op0=ALU.mult,
                                     op1=ALU.min).then_inc(distance, 1)
            dve.wait_ge(distance, 1)
            for n in range(7):
                dve.tensor_scalar(tables[:, n], e[:, 1, 0], float(DILATIONS[n // 3]), None, ALU.mult)\
                   .then_inc(distance, 1)
            for n in range(4):
                dve.memset(slope[:, n:n + 1], 2.0 ** -(n + 1)).then_inc(slope_set, 1)
            for item in range(4):
                dve.wait_ge(hi_made, item + 1)
                if item < 2:
                    low = q_parts[HD:P, 0, item]
                    dve.tensor_tensor(low, first_raw[item][HD:P, :], low.bitcast(F32), ALU.subtract).then_inc(parts_made, 1)
                else:
                    at = slice(PAD, PAD + S)
                    dve.tensor_tensor(k_lo[:, 0, item % 2, at], first_raw[item], k_hi[:, 0, item % 2, at].bitcast(F32),
                                      ALU.subtract).then_inc(parts_made, 1)
            dve.wait_ge(masked, 18)
            dve.wait_ge(slope_set, 4)
            dve.wait_ge(distance, 8)

            with dve.Fori(0, 2) as i:
                def bias_and_top(u):
                    n = UPT * i + u
                    d, cls, b, _ = units[u % UPP]
                    last = NT // d - 1
                    if d == NT:
                        table, src = tables[:, 6, REACH:REACH + P], slice((cls % 2) * P, (cls % 2 + 1) * P)
                    else:
                        table = tables[:, 3 * DILATIONS.index(d) + (1 if b == 0 else 2 if b == last else 0)]
                        src = slice(0, WIN)
                    w = src.stop - src.start
                    dve.wait_ge(scored, n + 1)
                    dve.wait_ge(turned, UPT * i + max(u - 3, 0))
                    dve.wait_ge(stored[u % 8], 16 * (UPT // 8 * i + u // 8))
                    dve.sem_inc(passed, 1)
                    for h in range(2):
                        at = slice(h * WIN + src.start, h * WIN + src.stop)
                        s = 2 * (u // UPP) + h
                        ins = dve.tensor_tensor_reduce(e[:, u % 4, h, 0:w], score[:, u % 4, at], table,
                                                       slope[:, s:s + 1], LOWEST, ALU.add, ALU.max,
                                                       top[:, u % 4, h:h + 1])
                        ins.then_inc(score_read, 1)
                    dve.wait_ge(score_read, 2 * n + 2)
                    dve.tensor_scalar(stage[:, u % 8, 2 * HD:2 * HD + 2], top[:, u % 4], -1.0, None, ALU.mult)\
                       .then_inc(top_made, 1)

                def move(u):
                    n = UPT * i + u
                    w = 4 if units[u % UPP][0] < NT else 2
                    dve.wait_ge(turned, n + 1)
                    dve.wait_ge(valued, UPT * i + max(u - 1, 0))
                    dve.tensor_copy(e_t[:, u % 2, 0:w], turn[:, u % 2, 0:w * P].rearrange("p (b n) -> p b n", n=P))\
                       .then_inc(moved[u % 2], 1)

                def move_out(u):
                    dve.wait_ge(valued, UPT * i + u + 1)
                    own = out[:, u % 2, 0:2 * (P + HD)].rearrange("p (h n) -> p h n", h=2)[:, :, 0:HD]
                    dve.tensor_copy(stage[:, u % 8, 0:2 * HD].rearrange("p (h n) -> p h n", h=2), own)\
                       .then_inc(staged, 1)

                for u in range(-3, UPT):
                    if u + 3 < UPT:
                        bias_and_top(u + 3)
                    if 0 <= u + 1 < UPT and (u + 1) % 2 == 1:
                        move(u + 1)
                    if u >= 0:
                        move_out(u)
                for n in range(4):
                    dve.tensor_scalar(slope[:, n:n + 1], slope[:, n:n + 1], 2.0 ** -4, None, ALU.mult)\
                       .then_inc(slope_set, 1)
                dve.wait_ge(slope_set, 4 * i + 8)

        @block.tensor
        def _(pe):
            with pe.Fori(0, 2) as i:
                def scores(u):
                    d, cls, b, _ = units[u % UPP]
                    par = u // UPP
                    if u % UPP == 0:
                        pe.wait_ge(parts_made, 8 * i + 4 * par + 4)
                    pe.wait_ge(score_read, 2 * UPT * i + 2 * max(u - 3, 0))
                    start = cls + d * P * b
                    for h in range(2):
                        q = q_parts[:, par, h, start:start + d * (P - 1) + 1:d]
                        for n, part in enumerate((k_hi, k_lo)):
                            if d == NT:
                                keys = part[:, par, h, PAD:PAD + S].rearrange("p (k c) -> p c k", c=NT)\
                                    [:, cls // 2 * 2:cls // 2 * 2 + 2]
                            else:
                                at = PAD + start - d * REACH
                                keys = part[:, par, h, at:at + d * (WIN - 1) + 1:d]
                            mm = pe.matmul(score[:, u % 4, h * WIN:(h + 1) * WIN], q, keys, start=(n == 0), stop=(n == 1))
                    mm.then_inc(scored, 1)

                def transposes(u):
                    n = UPT * i + u
                    pe.wait_ge(exped, 2 * n + 2)
                    pe.wait_ge(moved[u % 2], UPT // 2 * i + u // 2)
                    w = 2 if units[u % UPP][0] < NT else 1
                    for h in range(2):
                        for k in range(w):
                            mm = pe.transpose(turn[:, u % 2, (w * h + k) * P:(w * h + k + 1) * P],
                                              e[:, u % 4, h, k * P:(k + 1) * P], ident[:, :])
                    mm.then_inc(turned, 1)

                def values(u):
                    n, par = UPT * i + u, u // UPP
                    chunk = units[u % UPP][3]
                    w = 2 if units[u % UPP][0] < NT else 1
                    if u % UPP == 0:
                        pe.wait_ge(v_loaded[par], 16 * V_DMAS * (i + 1))
                    pe.wait_ge(moved[u % 2], UPT // 2 * i + u // 2 + 1)
                    pe.wait_ge(staged, UPT * i + max(u - 1, 0))
                    for h in range(2):
                        for k in range(w):
                            mm = pe.matmul(out[:, u % 2, h * P:(h + 1) * P], e_t[:, u % 2, w * h + k],
                                           v[:, par, chunk + k], start=(k == 0), stop=(k == w - 1))
                    mm.then_inc(valued, 1)

                for u in range(-3, UPT):
                    if u + 3 < UPT:
                        scores(u + 3)
                    if 0 <= u + 1 < UPT:
                        transposes(u + 1)
                    if u >= 0:
                        values(u)


def over_tiles(eng, body, straight=False, head=0):
    if straight:
        for t in range(NT):
            body(t, t // 2, t % 2, t + 1 < NT)
        return
    for t in range(2 * head):
        body(t, t // 2, t % 2, True)
    with eng.Fori(head, NT // 2 - 1) as i:
        body(2 * i, i, 0, True)
        body(2 * i + 1, i, 1, True)
    body(NT - 2, NT // 2 - 1, 0, True)
    body(NT - 1, NT // 2 - 1, 1, False)


def over_quads(eng, body, head=0):
    for t in range(4 * head):
        body(t, t // 2, t % 2, True, t // 4, t % 4)
    with eng.Fori(head, NT // 4 - 1) as turn:
        for slot in range(4):
            body(4 * turn + slot, 2 * turn + slot // 2, slot % 2, True, turn, slot)
    for slot in range(4):
        t = NT - 4 + slot
        body(t, t // 2, t % 2, t + 1 < NT, NT // 4 - 1, slot)


class Weights:

    SLOTS = 3

    def __init__(self, ph, matrices, pieces=None):
        self.parts, self.jobs = [], []
        for n, m in enumerate(matrices):
            kts = m.shape[0] // P
            hi = ph.sb(f"w{n}_hi", [P, kts, D], F32R)
            lo = ph.sb(f"w{n}_lo", [P, kts, D], F32R)
            self.parts.append((hi, lo))
            whole = [[(slice(0, P), m.rearrange("(kt p) n -> kt p n", p=P)[kt])] for kt in range(kts)]
            self.jobs += [(pieces(m, kt) if pieces else whole[kt], hi[:, kt], lo[:, kt]) for kt in range(kts)]
        self.raw = ph.sb("w_raw", [P, self.SLOTS, D])
        self.loaded = ph.sems("w_loaded", self.SLOTS)
        self.hi_made = ph.sem("w_hi_made")
        self.lo_made = ph.sems("w_lo_made", 2)
        self.total = len(self.jobs)

    def load(self, sp):
        for n, (src, _, _) in enumerate(self.jobs):
            if n >= self.SLOTS:
                sp.wait_ge(self.lo_made[(n - self.SLOTS) % 2], (n - self.SLOTS) // 2 + 1)
            for at, part in src:
                sp.dma_start(self.raw[at, n % self.SLOTS], part).then_inc(self.loaded[n % self.SLOTS], 16)

    def make_hi(self, act):
        for n, (src, hi, _) in enumerate(self.jobs):
            act.wait_ge(self.loaded[n % self.SLOTS], 16 * len(src) * (n // self.SLOTS + 1))
            act.activation(hi, self.raw[:, n % self.SLOTS], ACT.Copy).then_inc(self.hi_made, 1)

    def make_lo(self, eng, which):
        for n, (_, hi, lo) in enumerate(self.jobs):
            if n % 2 == which:
                eng.wait_ge(self.hi_made, n + 1)
                eng.tensor_tensor(lo, self.raw[:, n % self.SLOTS], hi.bitcast(F32), ALU.subtract)\
                   .then_inc(self.lo_made[which], 1)

    def wait_made(self, pe, upto=None):
        n = self.total if upto is None else upto
        pe.wait_ge(self.lo_made[0], (n + 1) // 2)
        pe.wait_ge(self.lo_made[1], n // 2)


def three_passes(pe, out, left, right, first, last):
    mm = pe.matmul(out, left[0], right[0], start=first, stop=False)
    mm = pe.matmul(out, left[0], right[1], start=False, stop=False)
    return pe.matmul(out, left[1], right[0], start=False, stop=last)


def merge_and_project(nc, c, x, sub_gain, w_out, cols, rows, a_t, ss_t, o_parts, x2, sq_sums):
    PAIRS = DIL_HEADS // 2
    HALF_W = D // 2
    x_t = x.rearrange("(t p) d -> t p d", p=P)
    x2_t = x2.rearrange("(t p) d -> t p d", p=P)
    a_v = a_t.rearrange("h p (t n) -> t p h n", n=P)
    ss_v = ss_t.rearrange("h p (t n) -> t p h n", n=P)
    za_v = cols[ZA:ZA + 4].rearrange("h p (t n) -> t p h n", n=P)
    zb_v = rows.rearrange("(t p) n -> t p n", p=P)
    o_v = [o.rearrange("(t p) a b -> t p (a b)", p=P) for o in o_parts]
    IN_DMAS = 7

    def two_more(t):
        return not isinstance(t, int) or t + 2 < NT

    with Phase(nc, "m") as ph:
        ident = c["ident"]
        w = Weights(ph, [w_out])
        a = ph.sb("a", [P, 2, 4, P])
        ss = ph.sb("ss", [P, 2, 4, P])
        za = ph.sb("za", [P, 2, 4, P])
        zb = ph.sb("zb", [P, 2, HALF_W])
        o = ph.sb("o", [P, 2, 3, PAIRS * PAIR_OUT])
        xt = ph.sb("xt", [P, 2, D])
        yb = ph.sb("yb", [P, 2, HALF_W])
        y_hi = ph.sb("y_hi", [P, 2, KT, P], F32R)
        y_lo = ph.sb("y_lo", [P, 2, KT, P], F32R)
        small = ph.sb("small", [P, 6, 3, DIL_HEADS])
        unused = ph.sb("unused", [P, D])
        gain = ph.sb("gain", [P, 2])
        turn = ph.banks("turn", 2)
        acc = ph.banks("acc", 4)

        in_loaded = ph.sems("in_loaded", 2)
        x_loaded = ph.sems("x_loaded", 2)
        gain_loaded = ph.sem("gain_loaded")
        gain_set = ph.sem("gain_set")
        rooted = ph.sem("rooted")
        diff_step = ph.sem("diff_step")
        dil_step = ph.sem("dil_step")
        exped = ph.sem("exped")
        scaled = ph.sem("scaled")
        merged = ph.sem("merged")
        yb_made = ph.sem("yb_made")
        a_hi_made = ph.sem("a_hi_made")
        a_lo_made = ph.sem("a_lo_made")
        turned = ph.sem("turned")
        b_hi_made = ph.sem("b_hi_made")
        b_lo_made = ph.sem("b_lo_made")
        weighed = ph.sem("weighed")
        projected = ph.sems("projected", 2)
        added = ph.sems("added", 2)
        squared = ph.sem("squared")
        stored = ph.sems("stored", 2)
        block = ph.block()

        @block.sync
        def _(sp):
            def load_in(t, par):
                arrived = in_loaded[par]
                sp.dma_start(ss[:, par], ss_v[t]).then_inc(arrived, 16)
                sp.dma_start(a[:, par], a_v[t]).then_inc(arrived, 16)
                sp.dma_start(za[:, par], za_v[t]).then_inc(arrived, 16)
                for n in range(3):
                    sp.dma_start(o[:, par, n], o_v[n][t]).then_inc(arrived, 16)
                sp.dma_start(zb[:, par], zb_v[t][:, ZB * P:ZB * P + HALF_W]).then_inc(arrived, 16)

            sp.dma_start(gain[:, 0:1], column(sub_gain), allow_slow_non_contiguous=True).then_inc(gain_loaded, 16)
            load_in(0, 0)
            load_in(1, 1)
            w.load(sp)
            sp.dma_start(xt[:, 0], x_t[0]).then_inc(x_loaded[0], 16)

            for t in range(NT + 1):
                if t + 2 < NT:
                    sp.wait_ge(a_lo_made, t + 1)
                    sp.wait_ge(yb_made, t + 1)
                    load_in(t + 2, t % 2)
                if t >= 1:
                    s = (t - 1) % 2
                    sp.wait_ge(added[s], (t - 1) // 2 + 1)
                    sp.dma_start(x2_t[t - 1], xt[:, s]).then_inc(stored[s], 16)
                if t + 1 < NT:
                    s = (t + 1) % 2
                    if t >= 1:
                        sp.wait_ge(stored[s], 16 * ((t - 1) // 2 + 1))
                        sp.wait_ge(squared, t)
                    sp.dma_start(xt[:, s], x_t[t + 1]).then_inc(x_loaded[s], 16)
            for s in range(2):
                sp.wait_ge(stored[s], 16 * NT // 2)

        def o_of(par, n):
            return o[:, par, n].rearrange("p (a b) -> p a b", b=PAIR_OUT)[:, :, 0:2 * HD]\
                .rearrange("p a (h e) -> p a h e", e=HD)

        def stat_of(par, k):
            at = 2 * HD + 2 * k
            return o[:, par].rearrange("p n (a b) -> p n a b", b=PAIR_OUT)[:, :, :, at:at + 2]

        def small_of(k, n=None):
            full = small[:, k].rearrange("p n (a h) -> p n a h", h=2)
            return full if n is None else full[:, n]

        @block.gpsimd
        def _(pool):
            def merge_dilated(t, i, par):
                pool.wait_ge(scaled, 3 * t + 3)
                pool.wait_ge(a_lo_made, t)
                mine = yb[:, par].rearrange("p (a h e) -> p a h e", a=PAIRS, h=2)
                pool.tensor_tensor(mine, o_of(par, 0), o_of(par, 1), ALU.add).then_inc(merged, 1)
                pool.wait_ge(merged, 2 * t + 1)
                pool.tensor_tensor(mine, mine, o_of(par, 2), ALU.add).then_inc(merged, 1)
                pool.wait_ge(merged, 2 * t + 2)
                pool.tensor_tensor(yb[:, par], yb[:, par], zb[:, par], ALU.mult).then_inc(yb_made, 1)

            def make_a_lo(t, i, par):
                pool.wait_ge(a_hi_made, t + 1)
                pool.wait_ge(yb_made, t + 1)
                pool.tensor_tensor(y_lo[:, par, 0:4], a[:, par], y_hi[:, par, 0:4].bitcast(F32), ALU.subtract)\
                    .then_inc(a_lo_made, 1)

            merge_dilated(0, 0, 0)
            make_a_lo(0, 0, 0)
            merge_dilated(1, 0, 1)
            w.make_lo(pool, 1)

            def body(t, i, par, more):
                if more:
                    make_a_lo(t + 1, i + par, 1 - par)
                if two_more(t):
                    pool.wait_ge(turned, t + 1)
                    merge_dilated(t + 2, i + 1, par)

            over_tiles(pool, body)

        @block.scalar
        def _(act):
            def exp_and_root(t, i, par):
                act.wait_ge(dil_step, 6 * t + 3)
                act.activation(small[:, 1], small[:, 0], ACT.Exp).then_inc(exped, 1)
                act.activation(ss[:, par], ss[:, par], ACT.Sqrt, scale=1.0 / P).then_inc(rooted, 1)

            def make_hi(t, i, par):
                act.wait_ge(diff_step, 3 * t + 3)
                act.wait_ge(projected[par], i)
                act.activation(y_hi[:, par, 0:4], a[:, par], ACT.Copy).then_inc(a_hi_made, 1)
                act.wait_ge(turned, t + 1)
                act.activation(y_hi[:, par, 4:8], turn[:, par].rearrange("p (b n) -> p b n", n=P), ACT.Copy)\
                   .then_inc(b_hi_made, 1)

            exp_and_root(0, 0, 0)
            make_hi(0, 0, 0)
            exp_and_root(1, 0, 1)
            w.make_hi(act)

            def body(t, i, par, more):
                if more:
                    make_hi(t + 1, i + par, 1 - par)
                if two_more(t):
                    exp_and_root(t + 2, i + 1, par)
                act.wait_ge(added[par], i + 1)
                act.wait_ge(squared, t)
                act.activation(unused[:, :], xt[:, par], ACT.Square, accum_out=sq_sums[:, t:t + 1] if isinstance(t, int)
                               else sq_sums[:, bass.ds(t, 1)]).then_inc(squared, 1)

            over_tiles(act, body)

        @block.vector
        def _(dve):
            dve.wait_ge(gain_loaded, 16)
            dve.tensor_scalar(gain[:, 1:2], gain[:, 0:1], 1.0 - LAM_INIT, None, ALU.mult).then_inc(gain_set, 1)
            dve.wait_ge(gain_set, 1)

            def weigh_dilated(t, i, par):
                dve.wait_ge(in_loaded[par], 16 * IN_DMAS * (i + 1))
                neg, tot = stat_of(par, 0), stat_of(par, 1)
                dve.tensor_tensor(small_of(2, 0), neg[:, 0], neg[:, 1], ALU.min).then_inc(dil_step, 1)
                dve.wait_ge(dil_step, 6 * t + 1)
                dve.tensor_tensor(small_of(2, 1), small_of(2, 0), neg[:, 2], ALU.min).then_inc(dil_step, 1)
                dve.wait_ge(dil_step, 6 * t + 2)
                for n in range(3):
                    ins = dve.tensor_tensor(small_of(0, n), small_of(2, 1), neg[:, n], ALU.subtract)
                ins.then_inc(dil_step, 1)
                dve.wait_ge(exped, t + 1)
                dve.tensor_tensor(small_of(3), small_of(1), tot, ALU.mult).then_inc(dil_step, 1)
                dve.wait_ge(dil_step, 6 * t + 4)
                dve.tensor_reduce(small[:, 4, 0], small[:, 3].rearrange("p n h -> p h n"), AX_X, ALU.add)\
                   .then_inc(dil_step, 1)
                dve.wait_ge(dil_step, 6 * t + 5)
                dve.reciprocal(small[:, 4, 1], small[:, 4, 0]).then_inc(dil_step, 1)
                dve.wait_ge(dil_step, 6 * t + 6)
                for n in range(3):
                    dve.tensor_tensor(small[:, 5, n], small[:, 1, n], small[:, 4, 1], ALU.mult).then_inc(weighed, 1)
                dve.wait_ge(weighed, 3 * t + 3)
                for n in range(3):
                    dve.tensor_tensor(o_of(par, n), o_of(par, n),
                                      small_of(5, n).unsqueeze(3).to_broadcast([P, PAIRS, 2, HD]), ALU.mult)\
                       .then_inc(scaled, 1)

            def norm_differential(t, i, par):
                dve.scalar_tensor_tensor(out=a[:, par], in0=a[:, par], scalar=gain[:, 1:2], in1=za[:, par],
                                         op0=ALU.mult, op1=ALU.mult).then_inc(diff_step, 1)
                dve.wait_ge(rooted, t + 1)
                dve.reciprocal(ss[:, par], ss[:, par]).then_inc(diff_step, 1)
                dve.wait_ge(diff_step, 3 * t + 2)
                dve.tensor_tensor(a[:, par], a[:, par], ss[:, par], ALU.mult).then_inc(diff_step, 1)
                dve.wait_ge(b_hi_made, t + 1)
                dve.tensor_tensor(y_lo[:, par, 4:8], turn[:, par].rearrange("p (b n) -> p b n", n=P),
                                  y_hi[:, par, 4:8].bitcast(F32), ALU.subtract).then_inc(b_lo_made, 1)

            weigh_dilated(0, 0, 0)
            norm_differential(0, 0, 0)
            weigh_dilated(1, 0, 1)
            w.make_lo(dve, 0)

            def body(t, i, par, more):
                if more:
                    norm_differential(t + 1, i + par, 1 - par)
                if two_more(t):
                    weigh_dilated(t + 2, i + 1, par)
                dve.wait_ge(projected[par], i + 1)
                dve.wait_ge(x_loaded[par], 16 * (i + 1))
                dve.tensor_tensor(xt[:, par], acc[:, 2 * par:2 * par + 2].rearrange("p a b -> p (a b)"), xt[:, par],
                                  ALU.add).then_inc(added[par], 1)

            over_tiles(dve, body)

        @block.tensor
        def _(pe):
            (w_hi, w_lo), = w.parts

            def transposes(t, par):
                pe.wait_ge(yb_made, t + 1)
                for b in range(4):
                    mm = pe.transpose(turn[:, par, b * P:(b + 1) * P], yb[:, par, b * P:(b + 1) * P], ident[:, :])
                mm.then_inc(turned, 1)

            def project(t, par, kts):
                for kt in kts:
                    if isinstance(t, int) and t == 0:
                        w.wait_made(pe, kt + 1)
                    for n in range(2):
                        at = slice(n * BANK, (n + 1) * BANK)
                        mm = three_passes(pe, acc[:, 2 * par + n], (y_hi[:, par, kt], y_lo[:, par, kt]),
                                          (w_hi[:, kt, at], w_lo[:, kt, at]), kt == 0, kt == KT - 1)
                return mm

            transposes(0, 0)

            def body(t, i, par, more):
                pe.wait_ge(a_lo_made, t + 1)
                pe.wait_ge(b_lo_made, t + 1)
                pe.wait_ge(added[par], i)
                project(t, par, range(0, 2))
                if more:
                    transposes(t + 1, 1 - par)
                project(t, par, range(2, KT)).then_inc(projected[par], 1)

            over_tiles(pe, body, head=1)


def gate_and_embed(nc, c, x2, sq_sums, norm_gain, w_gate, emb, w_proj, x3):
    E = emb.shape[1]
    ET = E // P
    x2_t = x2.rearrange("(t p) d -> t p d", p=P)
    x3_t = x3.rearrange("(t p) d -> t p d", p=P)
    emb_t = emb.rearrange("(t p) d -> t p d", p=P)

    with Phase(nc, "g") as ph:
        ident, eps = c["ident"], c["eps"]
        w = Weights(ph, [w_gate, w_proj])
        xt = ph.sb("xt", [P, 4, D])
        new = ph.sb("new", [P, 2, D])
        et = ph.sb("et", [P, 4, E])
        gain_all = ph.sb("gain_all", [P, D])
        h = ph.sb("h", [P, D])
        h_hi = ph.sb("h_hi", [P, 2, KT + ET, P], F32R)
        h_lo = ph.sb("h_lo", [P, 2, KT + ET, P], F32R)
        sig = ph.sb("sig", [P, D])
        inv = ph.sb("inv", [P, 2, NT])
        turn = ph.banks("turn", 3)
        gate = ph.banks("gate", 2)
        proj = ph.banks("proj", 2)

        gain_loaded = ph.sem("gain_loaded")
        x_loaded = ph.sems("x_loaded", 4)
        rooted = ph.sem("rooted")
        inverted = ph.sem("inverted")
        normed = ph.sem("normed")
        turned = ph.sem("turned")
        hi_made = ph.sem("hi_made")
        lo_made = ph.sem("lo_made")
        gated = ph.sem("gated")
        embedded = ph.sem("embedded")
        sig_made = ph.sem("sig_made")
        multiplied = ph.sem("multiplied")
        added = ph.sem("added")
        stored = ph.sems("stored", 2)
        block = ph.block()

        @block.sync
        def _(sp):
            def load(t):
                sp.dma_start(xt[:, t % 4], x2_t[t]).then_inc(x_loaded[t % 4], 16)
                sp.dma_start(et[:, t % 4], emb_t[t]).then_inc(x_loaded[t % 4], 16)

            load(0)
            sp.dma_start(gain_all[:, :], row_on_all(norm_gain, P)).then_inc(gain_loaded, 16)
            load(1)
            w.load(sp)
            load(2)
            load(3)
            for t in range(NT):
                sp.wait_ge(added, t + 1)
                if t + 4 < NT:
                    sp.wait_ge(turned, t + 1)
                    load(t + 4)
                sp.dma_start(x3_t[t], new[:, t % 2]).then_inc(stored[t % 2], 16)
            for s in range(2):
                sp.wait_ge(stored[s], 16 * NT // 2)

        @block.gpsimd
        def _(pool):
            w.make_lo(pool, 1)

        @block.scalar
        def _(act):
            act.activation(inv[:, 0], sq_sums[:, :], ACT.Sqrt, bias=eps[:, 0:1], scale=1.0 / D).then_inc(rooted, 1)
            def prepare(t, i, par):
                act.wait_ge(turned, t + 1)
                act.activation(h_hi[:, par], turn[:, :].rearrange("p a (b n) -> p (a b) n", n=P)[:, 0:KT + ET],
                               ACT.Copy).then_inc(hi_made, 1)

            prepare(0, 0, 0)
            w.make_hi(act)

            def body(t, i, par, more):
                if more:
                    prepare(t + 1, i + par, 1 - par)
                act.wait_ge(gated, t + 1)
                act.wait_ge(multiplied, t)
                act.activation(sig[:, :], gate[:, :].rearrange("p a b -> p (a b)"), ACT.Sigmoid).then_inc(sig_made, 1)

            over_tiles(act, body)

        @block.vector
        def _(dve):
            dve.wait_ge(rooted, 1)
            dve.reciprocal(inv[:, 1], inv[:, 0]).then_inc(inverted, 1)
            dve.wait_ge(gain_loaded, 16)
            dve.wait_ge(inverted, 1)

            def norm(t, turn, slot):
                dve.wait_ge(x_loaded[slot], 32 * (turn + 1))
                dve.wait_ge(turned, t)
                scale = inv[:, 1, t:t + 1] if isinstance(t, int) else inv[:, 1, bass.ds(t, 1)]
                dve.scalar_tensor_tensor(out=h[:, :], in0=xt[:, slot], scalar=scale, in1=gain_all[:, :],
                                         op0=ALU.mult, op1=ALU.mult).then_inc(normed, 1)

            def make_lo(t, i, par):
                dve.wait_ge(hi_made, t + 1)
                dve.tensor_tensor(h_lo[:, par], turn[:, :].rearrange("p a (b n) -> p (a b) n", n=P)[:, 0:KT + ET],
                                  h_hi[:, par].bitcast(F32), ALU.subtract).then_inc(lo_made, 1)

            norm(0, 0, 0)
            make_lo(0, 0, 0)
            w.make_lo(dve, 0)

            def body(t, i, par, more, turn, slot):
                if more:
                    norm(t + 1, turn + (slot + 1) // 4, (slot + 1) % 4)
                    make_lo(t + 1, i + par, 1 - par)
                dve.wait_ge(embedded, t + 1)
                dve.wait_ge(sig_made, t + 1)
                dve.wait_ge(stored[par], 16 * i)
                dve.tensor_tensor(new[:, par], proj[:, :].rearrange("p a b -> p (a b)"), sig[:, :], ALU.mult)\
                   .then_inc(multiplied, 1)
                dve.wait_ge(multiplied, t + 1)
                dve.tensor_tensor(new[:, par], new[:, par], xt[:, slot], ALU.add).then_inc(added, 1)

            over_quads(dve, body)

        @block.tensor
        def _(pe):
            (g_hi, g_lo), (p_hi, p_lo) = w.parts

            def transposes(t, slot):
                pe.wait_ge(normed, t + 1)
                pe.wait_ge(lo_made, t)
                for k in range(KT + ET):
                    src = h[:, k * P:(k + 1) * P] if k < KT else et[:, slot, (k - KT) * P:(k - KT + 1) * P]
                    mm = pe.transpose(turn[:, k // 4, (k % 4) * P:(k % 4 + 1) * P], src, ident[:, :])
                mm.then_inc(turned, 1)

            def project(t, out, par, first, w_parts, kts, n_kts):
                for kt in kts:
                    if isinstance(t, int) and t == 0:
                        w.wait_made(pe, first + kt + 1)
                    for n in range(2):
                        at = slice(n * BANK, (n + 1) * BANK)
                        mm = three_passes(pe, out[:, n], (h_hi[:, par, first + kt], h_lo[:, par, first + kt]),
                                          (w_parts[0][:, kt, at], w_parts[1][:, kt, at]), kt == 0, kt == n_kts - 1)
                return mm

            transposes(0, 0)

            def body(t, i, par, more, turn, slot):
                pe.wait_ge(lo_made, t + 1)
                pe.wait_ge(sig_made, t)
                project(t, gate, par, 0, (g_hi, g_lo), range(0, 5), KT)
                if more:
                    transposes(t + 1, (slot + 1) % 4)
                project(t, gate, par, 0, (g_hi, g_lo), range(5, KT), KT).then_inc(gated, 1)
                pe.wait_ge(multiplied, t)
                project(t, proj, par, KT, (p_hi, p_lo), range(ET), ET).then_inc(embedded, 1)

            over_quads(pe, body, head=1)


Q_HEADS = 16
KV_HEADS = 4
GROUP = Q_HEADS // KV_HEADS
BUCKETS = 32
SPREAD = 3 * P
SQ, SK, SV, SZ = 0, 8, 10, 12


def bucket_choice():
    exact = BUCKETS // 2
    dist = np.maximum(2 * P - 1 - np.arange(SPREAD), 0)
    log = np.log(np.maximum(dist, 1).astype(np.float32) / np.float32(exact)) / np.float32(math.log(P / exact))
    large = np.minimum(exact + (log * np.float32(BUCKETS - exact)).astype(np.int32), BUCKETS - 1)
    bucket = np.where(dist < exact, dist, large)
    return (bucket[None, :] == np.arange(BUCKETS)[:, None]).astype(np.float32)


def window_attention(nc, c, sinks, t5_table, choice, by_distance, cols, rows, y_t):
    WIN = 2 * P
    UPG = NT
    UPT = 2 * UPG
    ITEMS = GROUP + 1
    y_v = y_t.rearrange("(h e) s -> e h s", e=HD)
    rows_v = rows.rearrange("(t p) n -> p t n", p=P)

    with Phase(nc, "w") as ph:
        ident = c["ident"]
        raw = ph.sb("raw", [P, 2, S])
        q_parts = ph.sb("q_parts", [P, 2, GROUP, S], F32R)
        k_hi = ph.sb("k_hi", [P, 2, S], F32R)
        k_lo = ph.sb("k_lo", [P, 2, S], F32R)
        v = ph.sb("v", [P, 2, NT, HD])
        bucket_values = ph.sb("bucket_values", [BUCKETS, Q_HEADS])
        chosen = ph.sb("chosen", [BUCKETS, SPREAD])
        line = ph.sb("line", [Q_HEADS, SPREAD])
        skewed = ph.sb("skewed", [P, Q_HEADS, WIN])
        flip = ph.sb("flip", [P, P])
        tables = ph.sb("tables", [P, Q_HEADS, WIN])
        bias = ph.sb("bias", [P, 2, GROUP, WIN])
        sink = ph.sb("sink", [P, 2, GROUP])
        e = ph.sb("e", [P, 3, GROUP, WIN])
        e_t = ph.sb("e_t", [P, 2, 2, GROUP * P])
        top = ph.sb("top", [P, 2, GROUP])
        neg = ph.sb("neg", [P, 3, GROUP])
        total = ph.sb("total", [P, 3, GROUP])
        sunk = ph.sb("sunk", [P, 3, GROUP])
        inv = ph.sb("inv", [P, 3, GROUP])
        y = ph.sb("y", [HD, 4, GROUP * P])
        score = ph.banks("score", 4)
        turn = ph.banks("turn", 2)
        out = ph.banks("out", 2)

        buckets_loaded = ph.sem("buckets_loaded")
        flip_made = ph.sem("flip_made")
        line_picked = ph.sem("line_picked")
        line_made = ph.sem("line_made")
        line_masked = ph.sem("line_masked")
        line_stored = ph.sem("line_stored")
        skew_loaded = ph.sem("skew_loaded")
        flipped = ph.sem("flipped")
        tables_made = ph.sem("tables_made")
        raw_loaded = ph.sems("raw_loaded", 2)
        early_loaded = ph.sems("early_loaded", ITEMS - 2)
        v_loaded = ph.sems("v_loaded", 2)
        bias_loaded = ph.sems("bias_loaded", 2)
        hi_made = ph.sem("hi_made")
        parts_made = ph.sem("parts_made")
        scored = ph.sem("scored")
        passed = ph.sem("passed")
        score_read = ph.sem("score_read")
        highest = ph.sem("highest")
        neg_made = ph.sem("neg_made")
        sink_less = ph.sem("sink_less")
        exped = ph.sem("exped")
        summed = ph.sem("summed")
        inverted = ph.sem("inverted")
        scaled = ph.sem("scaled")
        turned = ph.sem("turned")
        moved_act = ph.sem("moved_act")
        moved_dve = ph.sem("moved_dve")
        valued = ph.sem("valued")
        staged = ph.sem("staged")
        stored = ph.sems("stored", 4)
        block = ph.block()
        first_raw = [raw[:, 0], raw[:, 1]] + [q_parts[:, 1, n].bitcast(F32) for n in range(ITEMS - 2)]

        def width(u):
            return 1 if u % UPG == 0 else 2

        @block.sync
        def _(sp):
            def load_raw(g, item):
                n = ITEMS * g + item
                to, arrived = raw[:, n % 2], raw_loaded[n % 2]
                if g == 0 and item >= 2:
                    to, arrived = first_raw[item], early_loaded[item - 2]
                elif g >= 1:
                    sp.wait_ge(parts_made, n - 1)
                row = SK * P + g * HD if item == 0 else SQ * P + (GROUP * g + item - 1) * HD
                for half in range(2):
                    sp.dma_start(to[half * HD:(half + 1) * HD, :], cols[row // P][row % P:row % P + HD, :])\
                      .then_inc(arrived, 16)

            def load_bias_and_values(g):
                if g >= 2:
                    sp.wait_ge(sink_less, UPG * (g - 1))
                    sp.wait_ge(valued, UPG * (g - 1))
                at = slice(GROUP * g, GROUP * (g + 1))
                arrived = bias_loaded[g % 2]
                sp.wait_ge(tables_made, 2 * (g + 1))
                sp.dma_start(bias[:, g % 2], tables[:, at]).then_inc(arrived, 16)
                sp.dma_start(sink[:, g % 2], row_on_all(sinks[at], P)).then_inc(arrived, 16)
                sp.dma_start(v[:, g % 2], rows_v[:, :, SV * P + g * HD:SV * P + (g + 1) * HD])\
                  .then_inc(v_loaded[g % 2], 16)

            sp.dma_start(bucket_values[:, :], t5_table).then_inc(buckets_loaded, 16)
            sp.dma_start(chosen[:, :], choice).then_inc(buckets_loaded, 16)
            load_raw(0, 0)
            load_raw(0, 1)
            sp.wait_ge(line_masked, 2)
            sp.dma_start(by_distance, line[:, :]).then_inc(line_stored, 16)
            load_raw(0, 2)
            sp.wait_ge(line_stored, 16)
            windows = bass.AP(by_distance.tensor, by_distance.offset, [[1, P], [SPREAD, Q_HEADS], [1, WIN]])
            sp.dma_start(skewed[:, :, :], windows).then_inc(skew_loaded, 16)
            for item in range(3, ITEMS):
                load_raw(0, item)
            load_raw(1, 0)
            load_raw(1, 1)
            load_bias_and_values(0)
            load_bias_and_values(1)
            raw_loads = {}
            for to in range(1, KV_HEADS):
                for item, ahead in enumerate((18, 16, 13, 10, 7)):
                    if UPG * to > ahead:
                        raw_loads.setdefault(UPG * to - ahead, []).append((to, item))
            for g in range(KV_HEADS):
                for t in range(NT):
                    u = UPG * g + t
                    for to, item in raw_loads.get(u, []):
                        load_raw(to, item)
                    if 1 <= g < KV_HEADS - 1 and t == 3:
                        load_bias_and_values(g + 1)
                    sp.wait_ge(staged, u + 1)
                    sp.dma_start(y_v[:, GROUP * g:GROUP * (g + 1), t * P:(t + 1) * P],
                                 y[:, u % 4].rearrange("p (h n) -> p h n", h=GROUP)).then_inc(stored[u % 4], 16)
            for s in range(4):
                sp.wait_ge(stored[s], 16 * KV_HEADS * NT // 4)

        @block.gpsimd
        def _(pool):
            pool.memset(flip[:, :], 0.0).then_inc(flip_made, 1)
            pool.wait_ge(flip_made, 1)
            pool.affine_select(out=flip[:, :], in_=flip[:, :], compare_op=ALU.not_equal, fill=1.0,
                               base=-(P - 1), pattern=[[1, P]], channel_multiplier=1).then_inc(flip_made, 1)
            for g in range(1, KV_HEADS):
                if g >= 2:
                    pool.wait_ge(scored, UPG * (g - 1))
                for item in range(ITEMS):
                    n = ITEMS * g + item
                    pool.wait_ge(raw_loaded[n % 2], 32 * ((n - ITEMS) // 2 + 2))
                    pool.wait_ge(parts_made, n)
                    hi = k_hi[:, g % 2] if item == 0 else q_parts[:, g % 2, item - 1]
                    pool.tensor_copy(hi, raw[:, n % 2]).then_inc(hi_made, 1)
                    pool.wait_ge(hi_made, n + 1)
                    if item == 0:
                        pool.tensor_tensor(k_lo[:, g % 2], raw[:, n % 2], hi.bitcast(F32), ALU.subtract)\
                            .then_inc(parts_made, 1)
                    else:
                        low = q_parts[HD:P, g % 2, item - 1]
                        pool.tensor_tensor(low, raw[HD:P, n % 2], low.bitcast(F32), ALU.subtract)\
                            .then_inc(parts_made, 1)

        @block.scalar
        def _(act):
            for n in range(ITEMS):
                act.wait_ge((raw_loaded + early_loaded)[n], 32)
                hi = k_hi[:, 0] if n == 0 else q_parts[:, 0, n - 1]
                act.activation(hi, first_raw[n], ACT.Copy).then_inc(hi_made, 1)

            with act.Fori(0, KV_HEADS // 2) as i:
                def exp(u):
                    n = UPT * i + u
                    w = width(u) * P
                    act.wait_ge(neg_made, n + 1)
                    for h in range(GROUP):
                        act.activation(e[:, u % 3, h, 0:w], e[:, u % 3, h, 0:w], ACT.Exp,
                                       bias=neg[:, u % 3, h:h + 1], accum_out=total[:, u % 3, h:h + 1])\
                           .then_inc(exped, 1)
                    act.wait_ge(sink_less, n + 1)
                    act.activation(sunk[:, u % 3], sunk[:, u % 3], ACT.Exp).then_inc(exped, 1)

                def move(u):
                    n = UPT * i + u
                    act.wait_ge(turned, n + 1)
                    act.wait_ge(valued, UPT * i + max(u - 1, 0))
                    act.activation(e_t[:, u % 2, 0], turn[:, 0], ACT.Copy).then_inc(moved_act, 1)

                def move_out(u):
                    act.wait_ge(valued, UPT * i + u + 1)
                    act.wait_ge(stored[u % 4], 16 * (UPT // 4 * i + u // 4))
                    act.activation(y[:, u % 4], out[0:HD, u % 2], ACT.Copy).then_inc(staged, 1)

                for u in range(-3, UPT):
                    if 0 <= u + 2 < UPT:
                        exp(u + 2)
                    if u >= 0:
                        move_out(u)
                    if 0 <= u + 1 < UPT:
                        move(u + 1)

        @block.vector
        def _(dve):
            dve.wait_ge(line_picked, 1)
            dve.tensor_copy(line[:, :], turn[0:Q_HEADS, 0, 0:SPREAD]).then_inc(line_made, 1)
            dve.wait_ge(line_made, 1)
            dve.memset(line[:, 0:P], MASKED).then_inc(line_masked, 1)
            dve.memset(line[:, 2 * P:3 * P], MASKED).then_inc(line_masked, 1)
            for n in range(ITEMS):
                dve.wait_ge(hi_made, n + 1)
                if n == 0:
                    dve.tensor_tensor(k_lo[:, 0], raw[:, 0], k_hi[:, 0].bitcast(F32), ALU.subtract)\
                       .then_inc(parts_made, 1)
                else:
                    low = q_parts[HD:P, 0, n - 1]
                    dve.tensor_tensor(low, first_raw[n][HD:P, :], low.bitcast(F32), ALU.subtract).then_inc(parts_made, 1)

            for n in range(8):
                dve.wait_ge(flipped, n + 1)
                dve.tensor_copy(tables[:, 2 * n:2 * n + 2].rearrange("p h n -> p (h n)"), score[:, n % 4])\
                   .then_inc(tables_made, 1)

            with dve.Fori(0, KV_HEADS // 2) as i:
                def bias_and_top(u):
                    n = UPT * i + u
                    par, w = u // UPG, width(u) * P
                    if u % UPG == 0:
                        dve.wait_ge(bias_loaded[par], 32 * (i + 1))
                    dve.wait_ge(scored, n + 1)
                    dve.wait_ge(turned, UPT * i + max(u - 2, 0))
                    dve.wait_ge(exped, (GROUP + 1) * (UPT * i + max(u - 2, 0)))
                    dve.sem_inc(passed, 1)
                    for h in range(GROUP):
                        bank = 2 * (u % 2) + h // 2
                        at = (h % 2) * WIN
                        dve.tensor_tensor_reduce(e[:, u % 3, h, 0:w], score[:, bank, at:at + w],
                                                 bias[:, par, h, WIN - w:WIN], 1.0, LOWEST, ALU.add, ALU.max,
                                                 top[:, u % 2, h:h + 1]).then_inc(score_read, 1)

                def small_steps(u, v):
                    if u < UPT:
                        dve.wait_ge(score_read, GROUP * (UPT * i + u + 1))
                        dve.tensor_tensor(sunk[:, u % 3], top[:, u % 2], sink[:, u // UPG], ALU.max).then_inc(highest, 1)
                    if 0 <= v < UPT:
                        dve.wait_ge(exped, (GROUP + 1) * (UPT * i + v + 1))
                        dve.tensor_tensor(total[:, v % 3], total[:, v % 3], sunk[:, v % 3], ALU.add).then_inc(summed, 1)
                    if u < UPT:
                        dve.wait_ge(highest, UPT * i + u + 1)
                        dve.tensor_scalar(neg[:, u % 3], sunk[:, u % 3], -1.0, None, ALU.mult).then_inc(neg_made, 1)
                    if 0 <= v < UPT:
                        dve.wait_ge(summed, UPT * i + v + 1)
                        dve.reciprocal(inv[:, v % 3], total[:, v % 3]).then_inc(inverted, 1)
                    if u < UPT:
                        dve.wait_ge(neg_made, UPT * i + u + 1)
                        dve.tensor_tensor(sunk[:, u % 3], sink[:, u // UPG], neg[:, u % 3], ALU.add)\
                           .then_inc(sink_less, 1)

                def scale(u):
                    w = width(u) * P
                    dve.wait_ge(inverted, UPT * i + u + 1)
                    own = e[:, u % 3, :, 0:w]
                    dve.tensor_tensor(own, own, inv[:, u % 3].unsqueeze(2).to_broadcast([P, GROUP, w]), ALU.mult)\
                       .then_inc(scaled, 1)

                def move(u):
                    n = UPT * i + u
                    dve.wait_ge(turned, n + 1)
                    dve.wait_ge(valued, UPT * i + max(u - 1, 0))
                    if width(u) == 2:
                        dve.tensor_copy(e_t[:, u % 2, 1], turn[:, 1]).then_inc(moved_dve, 1)

                for u in range(-3, UPT):
                    if 0 <= u + 1 < UPT:
                        scale(u + 1)
                    if u + 3 < UPT:
                        bias_and_top(u + 3)
                    small_steps(u + 3, u + 2)
                    if 0 <= u + 1 < UPT:
                        move(u + 1)

        @block.tensor
        def _(pe):
            pe.wait_ge(buckets_loaded, 32)
            pe.matmul(turn[0:Q_HEADS, 0, 0:SPREAD], bucket_values[:, :], chosen[:, :], start=True, stop=True)\
              .then_inc(line_picked, 1)
            pe.wait_ge(flip_made, 2)
            pe.wait_ge(skew_loaded, 16)
            for n in range(8):
                if n >= 4:
                    pe.wait_ge(tables_made, n - 3)
                pe.matmul(score[:, n % 4], flip[:, :], skewed[:, 2 * n:2 * n + 2].rearrange("p h n -> p (h n)"),
                          start=True, stop=True).then_inc(flipped, 1)
            pe.wait_ge(tables_made, 8)

            with pe.Fori(0, KV_HEADS // 2) as i:
                def seconds(u):
                    return (UPT - 2) * i + u - (1 if u > 0 else 0) - (1 if u > UPG else 0)

                def scores(u):
                    par, t = u // UPG, u % UPG
                    w = width(u) * P
                    if t == 0:
                        pe.wait_ge(parts_made, 2 * ITEMS * i + ITEMS * (par + 1))
                    pe.wait_ge(score_read, GROUP * (UPT * i + max(u - 1, 0)))
                    keys = slice((t + 1) * P - w, (t + 1) * P)
                    for h in range(GROUP):
                        at = (h % 2) * WIN
                        for n, part in enumerate((k_hi, k_lo)):
                            mm = pe.matmul(score[:, 2 * (u % 2) + h // 2, at:at + w],
                                           q_parts[:, par, h, t * P:(t + 1) * P], part[:, par, keys],
                                           start=(n == 0), stop=(n == 1))
                    mm.then_inc(scored, 1)

                def transposes(u):
                    n = UPT * i + u
                    pe.wait_ge(scaled, n + 1)
                    pe.wait_ge(moved_act, n)
                    pe.wait_ge(moved_dve, seconds(u))
                    for k in range(width(u)):
                        for h in range(GROUP):
                            mm = pe.transpose(turn[:, k, h * P:(h + 1) * P], e[:, u % 3, h, k * P:(k + 1) * P],
                                              ident[:, :])
                    mm.then_inc(turned, 1)

                def values(u):
                    n, par, t = UPT * i + u, u // UPG, u % UPG
                    w = width(u)
                    if t == 0:
                        pe.wait_ge(v_loaded[par], 16 * (i + 1))
                    pe.wait_ge(moved_act, n + 1)
                    pe.wait_ge(moved_dve, seconds(u + 1))
                    pe.wait_ge(staged, UPT * i + max(u - 1, 0))
                    for k in range(w):
                        mm = pe.matmul(out[0:HD, u % 2], v[:, par, t - (w - 1) + k], e_t[:, u % 2, k],
                                       start=(k == 0), stop=(k == w - 1))
                    mm.then_inc(valued, 1)

                for u in range(-3, UPT):
                    if u + 3 < UPT:
                        scores(u + 3)
                    if u >= 0:
                        values(u)
                    if 0 <= u + 1 < UPT:
                        transposes(u + 1)


def project_and_norm(nc, c, x3, y_t, cols, w_out, final_gain, result):
    x_t = x3.rearrange("(t p) d -> t p d", p=P)
    res_t = result.rearrange("(t p) d -> t p d", p=P)
    y_v = y_t.rearrange("(kt p) (t n) -> t p kt n", p=P, n=P)
    z_v = cols[SZ:SZ + KT].rearrange("kt p (t n) -> t p kt n", n=P)

    with Phase(nc, "f") as ph:
        eps = c["eps"]
        w = Weights(ph, [w_out])
        y = ph.sb("y", [P, 2, KT, P])
        z = ph.sb("z", [P, 2, KT, P])
        y_hi = ph.sb("y_hi", [P, 2, KT, P], F32R)
        y_lo = ph.sb("y_lo", [P, 2, KT, P], F32R)
        xt = ph.sb("xt", [P, 2, D])
        new = ph.sb("new", [P, 2, D])
        unused = ph.sb("unused", [P, D])
        gain_all = ph.sb("gain_all", [P, D])
        stat = ph.sb("stat", [P, 2, 3])
        acc = ph.banks("acc", 4)

        y_loaded = ph.sems("y_loaded", 2)
        x_loaded = ph.sems("x_loaded", 2)
        gain_loaded = ph.sem("gain_loaded")
        gated = ph.sem("gated")
        y_hi_made = ph.sem("y_hi_made")
        y_lo_made = ph.sem("y_lo_made")
        projected = ph.sem("projected")
        added = ph.sems("added", 2)
        squared = ph.sem("squared")
        rooted = ph.sem("rooted")
        inverted = ph.sem("inverted")
        normed = ph.sem("normed")
        stored = ph.sems("stored", 2)
        block = ph.block()

        @block.sync
        def _(sp):
            def load(t):
                sp.dma_start(y[:, t % 2], y_v[t]).then_inc(y_loaded[t % 2], 16)
                sp.dma_start(z[:, t % 2], z_v[t]).then_inc(y_loaded[t % 2], 16)

            def load_x(t):
                sp.dma_start(xt[:, t % 2], x_t[t]).then_inc(x_loaded[t % 2], 16)

            load(0)
            w.load(sp)
            load(1)
            load_x(0)
            load_x(1)
            sp.dma_start(gain_all[:, :], row_on_all(final_gain, P)).then_inc(gain_loaded, 16)
            for t in range(NT):
                if t + 2 < NT:
                    sp.wait_ge(y_lo_made, t + 1)
                    load(t + 2)
                    sp.wait_ge(added[t % 2], t // 2 + 1)
                    load_x(t + 2)
                sp.wait_ge(normed, t + 1)
                sp.dma_start(res_t[t], new[:, t % 2]).then_inc(stored[t % 2], 16)
            for s in range(2):
                sp.wait_ge(stored[s], 16 * NT // 2)

        @block.gpsimd
        def _(pool):
            def make_lo(t, i, par):
                pool.wait_ge(y_hi_made, t + 1)
                pool.tensor_tensor(y_lo[:, par], y[:, par], y_hi[:, par].bitcast(F32), ALU.subtract)\
                    .then_inc(y_lo_made, 1)

            make_lo(0, 0, 0)
            w.make_lo(pool, 1)

            def body(t, i, par, more):
                if more:
                    make_lo(t + 1, i + par, 1 - par)

            over_tiles(pool, body)

        @block.scalar
        def _(act):
            def make_hi(t, i, par):
                act.wait_ge(gated, t + 1)
                act.activation(y_hi[:, par], y[:, par], ACT.Copy).then_inc(y_hi_made, 1)

            make_hi(0, 0, 0)
            w.make_hi(act)

            def body(t, i, par, more):
                if more:
                    act.wait_ge(projected, t)
                    make_hi(t + 1, i + par, 1 - par)
                act.wait_ge(added[par], i + 1)
                act.wait_ge(squared, t)
                act.activation(unused[:, :], new[:, par], ACT.Square, accum_out=stat[:, par, 0:1]).then_inc(squared, 1)
                act.wait_ge(squared, t + 1)
                act.activation(stat[:, par, 1:2], stat[:, par, 0:1], ACT.Sqrt, bias=eps[:, 0:1], scale=1.0 / D)\
                   .then_inc(rooted, 1)

            over_tiles(act, body)

        @block.vector
        def _(dve):
            def gate(t, i, par):
                dve.wait_ge(y_loaded[par], 32 * (i + 1))
                dve.tensor_tensor(y[:, par], y[:, par], z[:, par], ALU.mult).then_inc(gated, 1)

            gate(0, 0, 0)
            w.make_lo(dve, 0)
            dve.wait_ge(gain_loaded, 16)

            def body(t, i, par, more):
                if more:
                    gate(t + 1, i + par, 1 - par)
                dve.wait_ge(projected, t + 1)
                dve.wait_ge(x_loaded[par], 16 * (i + 1))
                dve.wait_ge(stored[par], 16 * i)
                dve.tensor_tensor(new[:, par], acc[:, 2 * par:2 * par + 2].rearrange("p a b -> p (a b)"), xt[:, par],
                                  ALU.add).then_inc(added[par], 1)
                dve.wait_ge(rooted, t + 1)
                dve.reciprocal(stat[:, par, 2:3], stat[:, par, 1:2]).then_inc(inverted, 1)
                dve.wait_ge(inverted, t + 1)
                dve.scalar_tensor_tensor(out=new[:, par], in0=new[:, par], scalar=stat[:, par, 2:3],
                                         in1=gain_all[:, :], op0=ALU.mult, op1=ALU.mult).then_inc(normed, 1)

            over_tiles(dve, body)

        @block.tensor
        def _(pe):
            (w_hi, w_lo), = w.parts

            def body(t, i, par, more):
                pe.wait_ge(y_lo_made, t + 1)
                pe.wait_ge(added[par], i)
                for kt in range(KT):
                    if isinstance(t, int) and t == 0:
                        w.wait_made(pe, kt + 1)
                    for n in range(2):
                        at = slice(n * BANK, (n + 1) * BANK)
                        mm = three_passes(pe, acc[:, 2 * par + n], (y_hi[:, par, kt], y_lo[:, par, kt]),
                                          (w_hi[:, kt, at], w_lo[:, kt, at]), kt == 0, kt == KT - 1)
                mm.then_inc(projected, 1)

            over_tiles(pe, body, head=1)


INPUTS = ("x", "p", "mix_norm_g", "w_in", "diff_q_norm_g", "diff_k_norm_g", "lambda_q1", "lambda_k1", "lambda_q2",
          "lambda_k2", "diff_sub_norm_g", "dil_q_norm_g", "dil_k_norm_g", "w_out", "ple_norm_g", "w_ple_gate",
          "w_ple_proj", "t5_table_2", "norm_g_2", "final_g_2", "a_w_in_2", "a_sinks_2", "a_w_out_2")


def build(nc, a, choice, result):
    def scratch(name, *shape):
        return nc.dram_tensor(name, shape, F32, kind="Internal").ap()

    in_width, swa_width = a["w_in"].shape[1], a["a_w_in_2"].shape[1]
    cols, rows = scratch("cols", in_width // P, P, S), scratch("rows", S, in_width)
    a_t, ss_t = scratch("a_t", DIFF_HEADS, P, S), scratch("ss_t", DIFF_HEADS, P, S)
    o_parts = [scratch(f"o_parts{n}", S, DIL_HEADS // 2, PAIR_OUT) for n in range(3)]
    x2, x3 = scratch("x2", S, D), scratch("x3", S, D)
    cols2, rows2 = scratch("cols2", swa_width // P, P, S), scratch("rows2", S, swa_width)
    by_distance = scratch("by_distance", Q_HEADS, SPREAD)
    y_t = scratch("y_t", D, S)

    with Phase(nc, "k") as ph:
        c = constants(nc, ph)
        sq_sums = ph.sb("sq_sums", [P, NT])
        fill_constants(nc, c)
        projection(nc, "p", c, a["x"], a["mix_norm_g"], a["w_in"], IN_SEGMENTS, cols, rows,
                   qk=[a["diff_q_norm_g"], a["diff_k_norm_g"], a["dil_q_norm_g"], a["dil_k_norm_g"]])
        diff_attention(nc, c, [a[f"lambda_{n}"] for n in ("q1", "k1", "q2", "k2")], cols, rows, a_t, ss_t)
        dilated_attention(nc, c, cols, rows, o_parts)
        merge_and_project(nc, c, a["x"], a["diff_sub_norm_g"], a["w_out"], cols, rows, a_t, ss_t, o_parts, x2,
                          sq_sums)
        gate_and_embed(nc, c, x2, sq_sums, a["ple_norm_g"], a["w_ple_gate"], a["p"], a["w_ple_proj"], x3)
        projection(nc, "s", c, x3, a["norm_g_2"], a["a_w_in_2"], SWA_SEGMENTS, cols2, rows2)
        window_attention(nc, c, a["a_sinks_2"], a["t5_table_2"], choice, by_distance, cols2, rows2, y_t)
        project_and_norm(nc, c, x3, y_t, cols2, a["a_w_out_2"], a["final_g_2"], result)


def kernel(**inputs):
    import concourse.bacc as _bacc
    from concourse.bass_utils import run_bass_kernel_spmd as _run

    nc = _bacc.Bacc("TRN2", target_bir_lowering=False, num_devices=1)
    arrays, args = {}, {}
    for name in INPUTS:
        a = np.ascontiguousarray(inputs[name])
        arrays[f"in_{name}"] = a
        ap = nc.dram_tensor(f"in_{name}", a.shape, mybir.dt.from_np(a.dtype), kind="ExternalInput").ap()
        while len(ap.shape) > 1 and ap.shape[0] == 1:
            ap = ap[0]
        args[name] = ap
    arrays["choice"] = bucket_choice()
    choice = nc.dram_tensor("choice", arrays["choice"].shape, F32, kind="ExternalInput").ap()
    result = nc.dram_tensor("result", (1, S, D), F32, kind="ExternalOutput").ap()
    build(nc, args, choice, result[0])
    r = _run(nc, [arrays], core_ids=[0])
    return r.results[0]["result"]
```
